# Optimizing a Trainium2 kernel written in Bass

```python
import jax, jax.numpy as jnp
from jax import lax
import numpy as np

D_MODEL = 1024
BATCH = 1
SEQ = 256
DEPTH = 4

CHUNK = 64
N_MIXERS = 3
HEAD_DIM = 64
N_HEADS = D_MODEL // HEAD_DIM
FOX_BLOCK = 128
B_LEFT_CHUNKS = 8
REL_CLIP = 128
C_KV_HEADS = N_HEADS // 8
C_GROUP = N_HEADS // C_KV_HEADS
C_WINDOW = 128
C_LEFT_CHUNKS = C_WINDOW // CHUNK - 1
ROPE_THETA = 10000.0
D_FF = 2816
CONV_WIDTH = 3
PLE_DIM = 256
EPS = 1e-6
FORGET_BIAS = 4.0
N_A = (DEPTH + 2) // 3
N_B = (DEPTH + 1) // 3
N_C = DEPTH // 3

kernel_name = "hybrid_streaming_fox_relpos_swa_convffn"

def rms_norm(x, g):
    xf = x.astype(jnp.float32)
    y = xf * lax.rsqrt(jnp.mean(xf * xf, axis=-1, keepdims=True) + EPS)
    return (y * g.astype(jnp.float32)).astype(x.dtype)

def rope(x):
    S = x.shape[1]
    half = HEAD_DIM // 2
    inv = ROPE_THETA ** (-jnp.arange(half, dtype=jnp.float32) / half)
    ang = jnp.arange(S, dtype=jnp.float32)[:, None] * inv[None, :]
    cos = jnp.cos(ang)[None, :, None, :]
    sin = jnp.sin(ang)[None, :, None, :]
    xf = x.astype(jnp.float32)
    x1, x2 = xf[..., :half], xf[..., half:]
    return jnp.concatenate([x1 * cos - x2 * sin, x2 * cos + x1 * sin], axis=-1).astype(x.dtype)

def chunk_band(x, n_prev):
    B, S, H, Dh = x.shape
    nc = S // CHUNK
    xp = jnp.pad(x, ((0, 0), (n_prev * CHUNK, 0), (0, 0), (0, 0)))
    xc = xp.reshape(B, nc + n_prev, CHUNK, H, Dh)
    band = jnp.stack([xc[:, w:w + nc] for w in range(n_prev + 1)], axis=2)
    return band.reshape(B, nc, (n_prev + 1) * CHUNK, H, Dh)

def band_valid(nc, n_prev):
    c_idx = jnp.arange(nc)[:, None]
    w = jnp.arange((n_prev + 1) * CHUNK)[None, :] // CHUNK
    return c_idx - n_prev + w >= 0

def fox_mixer(h, w_in, b_f, qn, kn):
    B, S, D = h.shape
    proj = h @ w_in
    q = rms_norm(proj[..., :D].reshape(B, S, N_HEADS, HEAD_DIM), qn)
    k = rms_norm(proj[..., D:2 * D].reshape(B, S, N_HEADS, HEAD_DIM), kn)
    v = proj[..., 2 * D:3 * D].reshape(B, S, N_HEADS, HEAD_DIM)
    log_f = jax.nn.log_sigmoid((proj[..., 3 * D:] + b_f).astype(jnp.float32))
    cum = jnp.cumsum(log_f, axis=1).transpose(0, 2, 1)
    scale = HEAD_DIM ** -0.5
    outs = []
    for start in range(0, S, FOX_BLOCK):
        end = start + FOX_BLOCK
        s = jnp.einsum('bqhd,bkhd->bhqk', q[:, start:end], k[:, :end]).astype(jnp.float32) * scale
        s = s + cum[:, :, start:end, None] - cum[:, :, None, :end]
        mask = (start + jnp.arange(FOX_BLOCK))[:, None] >= jnp.arange(end)[None, :]
        s = jnp.where(mask, s, -jnp.inf)
        pr = jax.nn.softmax(s, axis=-1).astype(v.dtype)
        outs.append(jnp.einsum('bhqk,bkhd->bqhd', pr, v[:, :end]))
    return jnp.concatenate(outs, axis=1).reshape(B, S, D)

def chunk_relpos_mixer(h, w_in, rel_bias, qn, kn):
    B, S, D = h.shape
    nc = S // CHUNK
    L = (B_LEFT_CHUNKS + 1) * CHUNK
    proj = h @ w_in
    q = rms_norm(proj[..., :D].reshape(B, S, N_HEADS, HEAD_DIM), qn)
    k = rms_norm(proj[..., D:2 * D].reshape(B, S, N_HEADS, HEAD_DIM), kn)
    v = proj[..., 2 * D:].reshape(B, S, N_HEADS, HEAD_DIM)
    qc = q.reshape(B, nc, CHUNK, N_HEADS, HEAD_DIM)
    kb = chunk_band(k, B_LEFT_CHUNKS)
    vb = chunk_band(v, B_LEFT_CHUNKS)
    s = jnp.einsum('bcqhd,bckhd->bchqk', qc, kb).astype(jnp.float32) * (HEAD_DIM ** -0.5)
    rel = B_LEFT_CHUNKS * CHUNK + jnp.arange(CHUNK)[:, None] - jnp.arange(L)[None, :]
    idx = jnp.clip(rel, -REL_CLIP, REL_CLIP) + REL_CLIP
    bias = rel_bias[idx].astype(jnp.float32).transpose(2, 0, 1)
    s = s + bias[None, None]
    valid = band_valid(nc, B_LEFT_CHUNKS)
    s = jnp.where(valid[None, :, None, None, :], s, -jnp.inf)
    pr = jax.nn.softmax(s, axis=-1).astype(vb.dtype)
    return jnp.einsum('bchqk,bckhd->bcqhd', pr, vb).reshape(B, S, D)

def swa_sink_mixer(h, w_in, sinks, qn, kn):
    B, S, D = h.shape
    nc = S // CHUNK
    kvd = C_KV_HEADS * HEAD_DIM
    proj = h @ w_in
    q = rope(rms_norm(proj[..., :D].reshape(B, S, N_HEADS, HEAD_DIM), qn))
    k = rope(rms_norm(proj[..., D:D + kvd].reshape(B, S, C_KV_HEADS, HEAD_DIM), kn))
    v = proj[..., D + kvd:].reshape(B, S, C_KV_HEADS, HEAD_DIM)
    qc = q.reshape(B, nc, CHUNK, C_KV_HEADS, C_GROUP, HEAD_DIM)
    kb = chunk_band(k, C_LEFT_CHUNKS)
    vb = chunk_band(v, C_LEFT_CHUNKS)
    s = jnp.einsum('bcqngd,bcknd->bcngqk', qc, kb).astype(jnp.float32) * (HEAD_DIM ** -0.5)
    valid = band_valid(nc, C_LEFT_CHUNKS)
    s = jnp.where(valid[None, :, None, None, None, :], s, -jnp.inf)
    sink = jnp.broadcast_to(
        sinks.astype(jnp.float32).reshape(C_KV_HEADS, C_GROUP)[None, None, :, :, None, None],
        s.shape[:-1] + (1,))
    pr = jax.nn.softmax(jnp.concatenate([s, sink], axis=-1), axis=-1)[..., :-1].astype(vb.dtype)
    return jnp.einsum('bcngqk,bcknd->bcqngd', pr, vb).reshape(B, S, D)

def conv_ffn(h, w_up, conv_w, conv_b, w_down):
    u = h @ w_up
    u = lax.conv_general_dilated(
        u, conv_w[:, None, :], window_strides=(1,), padding=[(CONV_WIDTH - 1, 0)],
        dimension_numbers=('NWC', 'WIO', 'NWC'), feature_group_count=2 * D_FF) + conv_b
    gate, up = u[..., :D_FF], u[..., D_FF:]
    return (jax.nn.silu(gate) * up) @ w_down

def setup_inputs(seed: int = 0) -> dict:
    key = jax.random.key(seed)
    ks = jax.random.split(key, 24)
    f32 = jnp.float32
    D = D_MODEL
    nrm = lambda k, shape, s: jax.random.normal(k, shape, f32) * s
    gain = lambda k, shape: 1.0 + 0.05 * jax.random.normal(k, shape, f32)
    c_cols = D + 2 * C_KV_HEADS * HEAD_DIM
    return {
        "x": nrm(ks[0], (BATCH, SEQ, D), 1.0),
        "p": nrm(ks[1], (DEPTH, BATCH, SEQ, PLE_DIM), 1.0),
        "attn_norm": gain(ks[2], (DEPTH, D)),
        "w_in_a": nrm(ks[3], (N_A, D, 3 * D + N_HEADS), D ** -0.5),
        "b_f": FORGET_BIAS + 0.5 * jax.random.normal(ks[4], (N_A, N_HEADS), f32),
        "qn_a": gain(ks[5], (N_A, HEAD_DIM)),
        "kn_a": gain(ks[6], (N_A, HEAD_DIM)),
        "w_in_b": nrm(ks[7], (N_B, D, 3 * D), D ** -0.5),
        "rel_bias": nrm(ks[8], (N_B, 2 * REL_CLIP + 1, N_HEADS), 0.5),
        "qn_b": gain(ks[9], (N_B, HEAD_DIM)),
        "kn_b": gain(ks[10], (N_B, HEAD_DIM)),
        "w_in_c": nrm(ks[11], (N_C, D, c_cols), D ** -0.5),
        "sinks": nrm(ks[12], (N_C, N_HEADS), 0.5),
        "qn_c": gain(ks[13], (N_C, HEAD_DIM)),
        "kn_c": gain(ks[14], (N_C, HEAD_DIM)),
        "w_o": nrm(ks[15], (DEPTH, D, D), D ** -0.5),
        "ffn_norm": gain(ks[16], (DEPTH, D)),
        "w_up": nrm(ks[17], (DEPTH, D, 2 * D_FF), D ** -0.5),
        "conv_w": nrm(ks[18], (DEPTH, CONV_WIDTH, 2 * D_FF), CONV_WIDTH ** -0.5),
        "conv_b": nrm(ks[19], (DEPTH, 2 * D_FF), 0.01),
        "w_down": nrm(ks[20], (DEPTH, D_FF, D), D_FF ** -0.5),
        "ple_norm": gain(ks[21], (DEPTH, D)),
        "w_ple_gate": nrm(ks[22], (DEPTH, D, D), D ** -0.5),
        "w_ple_proj": nrm(ks[23], (DEPTH, PLE_DIM, D), PLE_DIM ** -0.5),
    }

def reference(x, p, attn_norm, w_in_a, b_f, qn_a, kn_a, w_in_b, rel_bias, qn_b, kn_b,
              w_in_c, sinks, qn_c, kn_c, w_o, ffn_norm, w_up, conv_w, conv_b, w_down,
              ple_norm, w_ple_gate, w_ple_proj):
    for i in range(DEPTH):
        m, j = i % N_MIXERS, i // N_MIXERS
        h = rms_norm(x, attn_norm[i])
        if m == 0:
            o = fox_mixer(h, w_in_a[j], b_f[j], qn_a[j], kn_a[j])
        elif m == 1:
            o = chunk_relpos_mixer(h, w_in_b[j], rel_bias[j], qn_b[j], kn_b[j])
        else:
            o = swa_sink_mixer(h, w_in_c[j], sinks[j], qn_c[j], kn_c[j])
        x = x + o @ w_o[i]
        x = x + conv_ffn(rms_norm(x, ffn_norm[i]), w_up[i], conv_w[i], conv_b[i], w_down[i])
        gate = jax.nn.sigmoid(rms_norm(x, ple_norm[i]) @ w_ple_gate[i])
        x = x + gate * (p[i] @ w_ple_proj[i])
    return x


_drawn_inputs = setup_inputs


def setup_inputs(seed=0):
    import zlib

    import numpy as np

    out = dict(_drawn_inputs(seed))
    spreads = {}
    factors = {'qn_a': 3.612,
     'kn_a': 4.14,
     'qn_b': 8.0,
     'kn_b': 8.0,
     'sinks': 8.0,
     'qn_c': 8.0,
     'kn_c': 8.0,
     'conv_b': 4.768,
     'ple_norm': 3.917}
    for name, (base, spread) in spreads.items():
        noise = np.random.default_rng([zlib.crc32(name.encode()), seed]).standard_normal(out[name].shape)
        drawn = base * np.exp(spread * noise) if base else spread * noise
        out[name] = __import__('jax').numpy.asarray(drawn.astype(out[name].dtype))
    for name, factor in factors.items():
        out[name] = (out[name] * factor).astype(out[name].dtype)
    return out
```

```python
from contextlib import ExitStack

import concourse.bass as bass
from concourse import mybir
import numpy as np

F32 = mybir.dt.float32
F32R = mybir.dt.float32r
ALU = mybir.AluOpType
ACT = mybir.ActivationFunctionType
AX = mybir.AxisListType

P = 128
D = 1024
SEQ = 256
DEPTH = 4
TT = SEQ // P
KC = D // P
HEADS = 16
HD = 64
D_FF = 2816
FC = D_FF // P
PLE = 256
EPS = 1e-6
CHUNK = 64
BIG = 1.0e30
FOX, REL, SWA = 0, 1, 2
MIXER = [i % 3 for i in range(DEPTH)]

UNIT = 2048
RING = 4
IN_UNITS = {FOX: 12, REL: 12, SWA: 5}
ROW_UNITS = 4
DOWN_UNITS = FC // 2

FIRST_IN, FIRST_O, FIRST_UP, FIRST_DOWN, FIRST_PLE, FIRST_GATE = [], [], [], [], [], []
_u = 0
for _m in MIXER:
    FIRST_IN.append(_u)
    FIRST_O.append(_u + IN_UNITS[_m])
    FIRST_UP.append(FIRST_O[-1] + ROW_UNITS)
    FIRST_DOWN.append(FIRST_UP[-1] + FC)
    FIRST_PLE.append(FIRST_DOWN[-1] + DOWN_UNITS)
    FIRST_GATE.append(FIRST_PLE[-1] + 1)
    _u = FIRST_GATE[-1] + ROW_UNITS
UNITS = _u

ITEMS = {FOX: 8, REL: 8, SWA: 6}
FIRST_ITEM = [sum(ITEMS[m] for m in MIXER[:i]) for i in range(DEPTH)]
VS = {FOX: 4, REL: 4, SWA: 2}
FIRST_V = [sum(VS[m] for m in MIXER[:i]) for i in range(DEPTH)]

C_ID, C_MASKA, C_MASKC, C_MASKB, C_TRI, C_COS, C_SIN, C_END = np.cumsum([0, 128, 384, 384, 64, 512, 64, 64]).tolist()
S_GAIN, S_BF, S_SINK, S_END = np.cumsum([0, DEPTH * 2 * HD, 2 * HEADS, HEADS]).tolist()


LAST_UNIT = [u for L in range(DEPTH) for u in (FIRST_UP[L] - 1, FIRST_PLE[L] - 1, FIRST_GATE[L] + ROW_UNITS - 1)]


def norm_event(n):
    return 4 * (n // 3) + (0, 2, 3)[n % 3]


class Chain:

    def __init__(self, engine, sem):
        self.engine, self.sem, self.n = engine, sem, 0

    def inc(self, ins):
        ins.then_inc(self.sem, 1)
        self.n += 1

    def wait(self):
        self.engine.wait_ge(self.sem, self.n)


def over_units(engine, first, count, body, peel=False):
    turns = count // RING
    at = [j for j in range(RING if peel else 0)]
    for j in at:
        body(first + j, (first + j) % RING, (first + j) // RING + 1, j)
    with engine.Fori(int(peel), turns) as i:
        for j in range(RING):
            u = first + j
            body(i * RING + u, u % RING, i + (u // RING + 1), i * RING + j)
    for j in range(turns * RING, count):
        u = first + j
        body(u, u % RING, u // RING + 1, j)


def trunk(nc, weights, x_in, p_in, gains, smalls, conv, wf_in, rel_in, sel_in, consts_in, out):
    with ExitStack() as ctx:
        sb = lambda name, shape, dt=F32, c=ctx: c.enter_context(nc.sbuf_tensor(name, shape, dt))
        sem = lambda name: ctx.enter_context(nc.semaphore(name))

        w_raw = sb("w_raw", [P, RING, UNIT])
        w_hi = sb("w_hi", [P, RING, UNIT], F32R)
        w_lo = sb("w_lo", [P, RING, UNIT], F32R)
        x = sb("x", [P, TT, D])
        tok = sb("tok", [P, TT, D])
        hT_hi = sb("hT_hi", [P, KC, SEQ], F32R)
        hT_lo = sb("hT_lo", [P, KC, SEQ], F32R)
        gain = sb("gain", [P, 2, D])
        consts = sb("consts", [P, C_END])
        small = sb("small", [P, S_END])
        nsink = sb("nsink", [P, HEADS])
        conv_sb = sb("conv_sb", [P, DEPTH, FC, 8])
        wf_raw = sb("wf_raw", [P, 2, KC, HEADS])
        wf_hi = sb("wf_hi", [P, 2, KC, HEADS], F32R)
        wf_lo = sb("wf_lo", [P, 2, KC, HEADS], F32R)
        p_raw = sb("p_raw", [P, 2, SEQ])
        p_hi = sb("p_hi", [P, 2, SEQ], F32R)
        p_lo = sb("p_lo", [P, 2, SEQ], F32R)
        ssq = sb("ssq", [P, TT])
        rstd = sb("rstd", [P, TT])
        hsum = sb("hsum", [P, 2, 8])
        hrstd = sb("hrstd", [P, 2, 8])
        neghalf = sb("neghalf", [P, 8])
        nmax = sb("nmax", [P, 2, HEADS])
        den = sb("den", [P, 2, HEADS])
        esink = sb("esink", [P, 2, HEADS])
        fz = sb("fz", [P, 2, HEADS])
        fe = sb("fe", [P, 2, HEADS])
        logf = sb("logf", [P, 2, HEADS])
        with ExitStack() as ffn:
            gT_hi = sb("gT_hi", [P, FC, SEQ], F32R, ffn)
            gT_lo = sb("gT_lo", [P, FC, SEQ], F32R, ffn)
            gate_c = sb("gate_c", [P, 2, SEQ], F32, ffn)
            up_c = sb("up_c", [P, 2, SEQ], F32, ffn)
        qT = sb("qT", [P, HEADS // 2, SEQ])
        kT = sb("kT", [P, HEADS // 2, SEQ])
        v = sb("v", [P, TT, D])
        sc = sb("sc", [P, 3, 3 * P])
        pT = sb("pT", [P, 2, 3 * P])
        cum_hi = sb("cum_hi", [HEADS, SEQ], F32R)
        cum_lo = sb("cum_lo", [HEADS, SEQ], F32R)
        with ExitStack() as only_fox:
            sel = sb("sel", [HEADS, HEADS, P], F32R, only_fox)
            sel_raw = sb("sel_raw", [HEADS, HEADS, P], F32, only_fox)
        with ExitStack() as only_swa:
            rope_c = sb("rope_c", [P, 512], F32, only_swa)
            rope_s = sb("rope_s", [P, 512], F32, only_swa)
            kdup = sb("kdup", [P, 2, 256], F32, only_swa)
        rel = sb("rel", [P, HEADS, SEQ])
        sq = tok[:, 0, :].rearrange("p (b n) -> p b n", b=2)
        qn = tok[:, 1, :].rearrange("p (b n) -> p b n", b=2)

        bank = [ctx.enter_context(nc.psum_tensor(f"bank{i}", [P, 512], F32)) for i in range(8)]
        acc, aux = bank[:4], bank[4:]

        ident = consts[:, C_ID:C_ID + P]
        maskA = consts[:, C_MASKA:C_MASKA + 384]
        maskC = consts[:, C_MASKC:C_MASKC + 384]
        maskB = consts[:, C_MASKB:C_MASKB + CHUNK]
        tri = consts[:, C_TRI:C_TRI + 512].rearrange("p (t s) -> p t s", t=TT)
        cos = consts[:, C_COS:C_COS + 64].rearrange("p (t s) -> p t s", t=TT)
        sin = consts[:, C_SIN:C_SIN + 64].rearrange("p (t s) -> p t s", t=TT)
        hgain = small[:, S_GAIN:S_BF].rearrange("p (l a d) -> p l a d", l=DEPTH, a=2)
        bf = small[:, S_BF:S_SINK].rearrange("p (l h) -> p l h", l=2)
        sink = small[:, S_SINK:S_END]

        raw_landed = [sem(f"raw_landed{i}") for i in range(RING)]
        hi_ready = sem("hi_ready")
        lo_ready = sem("lo_ready")
        unit_used = sem("unit_used")
        consts_landed = sem("consts_landed")
        x_landed = sem("x_landed")
        gain_landed = [sem("gain_landed0"), sem("gain_landed1")]
        p_landed = sem("p_landed")
        sel_landed = sem("sel_landed")
        rel_landed = sem("rel_landed")
        stored = sem("stored")
        setup_act = sem("setup_act")
        setup_pool = sem("setup_pool")
        wf_ready = sem("wf_ready")
        x_ready = sem("x_ready")
        ssq_ready = sem("ssq_ready")
        rstd_ready = sem("rstd_ready")
        hsum_ready = sem("hsum_ready")
        hrstd_ready = sem("hrstd_ready")
        tok_ready = sem("tok_ready")
        tr_done = sem("tr_done")
        hT_hi_ready = sem("hT_hi_ready")
        hT_ready = sem("hT_ready")
        tile_done = sem("tile_done")
        sq_ready = sem("sq_ready")
        qn_raw = sem("qn_raw")
        qn_ready = sem("qn_ready")
        qk_tr = sem("qk_tr")
        qkT_ready = sem("qkT_ready")
        v_ready = sem("v_ready")
        rel_ready = sem("rel_ready")
        sel_ready = sem("sel_ready")
        f_done = sem("f_done")
        f_z = sem("f_z")
        f_ln = sem("f_ln")
        logf_ready = sem("logf_ready")
        cum_done = sem("cum_done")
        cum_hi_ready = sem("cum_hi_ready")
        cum_ready = sem("cum_ready")
        s_done = sem("s_done")
        s_min = sem("s_min")
        p_ready = sem("p_ready")
        pt_done = sem("pt_done")
        pt_copied = sem("pt_copied")
        pv_done = sem("pv_done")
        esink_in = sem("esink_in")
        esink_ready = sem("esink_ready")
        conv_first = sem("conv_first")
        conv_tap = sem("conv_tap")
        conv_done = sem("conv_done")
        silu_done = sem("silu_done")
        prod_done = sem("prod_done")
        gT_hi_ready = sem("gT_hi_ready")
        gT_ready = sem("gT_ready")
        ps_hi = sem("ps_hi")
        ps_ready = sem("ps_ready")
        sg_ready = sem("sg_ready")
        dve_own = sem("dve_own")
        act_own = sem("act_own")
        pool_own = sem("pool_own")

        def wait_tile(engine, update, t):
            if t == 0:
                engine.wait_ge(tile_done, update + 1)
            else:
                engine.wait_ge(unit_used, LAST_UNIT[update] + 1)

        block = ctx.enter_context(nc.Block())

        @block.sync
        def _(sp):
            sp.dma_start(x[:], x_in.rearrange("(t p) d -> p t d", p=P)).then_inc(x_landed, 16)
            for u in range(RING):
                sp.dma_start(w_raw[:, u, :], weights[u]).then_inc(raw_landed[u], 16)
            turns = UNITS // RING
            with sp.Fori(1, turns) as i:
                for j in range(RING):
                    sp.wait_ge(lo_ready, i * RING + (j - RING + 1))
                    sp.dma_start(w_raw[:, j, :], weights[i * RING + j]).then_inc(raw_landed[j], 16)
            for u in range(turns * RING, UNITS):
                sp.wait_ge(lo_ready, u - RING + 1)
                sp.dma_start(w_raw[:, u % RING, :], weights[u]).then_inc(raw_landed[u % RING], 16)
            for t in range(TT):
                sp.wait_ge(x_ready, 2 * (3 * DEPTH - 1) + t + 1)
                sp.dma_start(out[t * P:(t + 1) * P, :], x[:, t, :]).then_inc(stored, 16)
            sp.wait_ge(stored, 16 * TT)

        @block.scalar
        def _(act):
            own = Chain(act, act_own)

            def split_hi(u, slot, turn, first=False):
                act.wait_ge(raw_landed[slot], turn * 16)
                if not first:
                    act.wait_ge(unit_used, u - (RING - 1))
                nc.scalar.activation(w_hi[:, slot, :], w_raw[:, slot, :], ACT.Copy).then_inc(hi_ready, 1)

            def split_next(u):
                if u + RING < UNITS:
                    split_hi(u + RING, u % RING, (u + RING) // RING + 1)

            def square(n, t):
                if n == 0:
                    act.wait_ge(x_landed, 16)
                else:
                    act.wait_ge(x_ready, 2 * (n - 1) + t + 1)
                nc.scalar.activation(tok[:, t, :], x[:, t, :], ACT.Square, scale=D ** -0.5,
                                     accum_out=ssq[:, t:t + 1]).then_inc(ssq_ready, 1)

            def round_hT(e, t, banks):
                for b in range(2):
                    act.wait_ge(tr_done, 4 * e + 2 * t + b + 1)
                    nc.scalar.activation(hT_hi[:, 4 * b:4 * b + 4, t * P:(t + 1) * P],
                                         banks[2 * t + b][:, :].rearrange("p (c s) -> p c s", c=4),
                                         ACT.Copy).then_inc(hT_hi_ready, 1)

            def norm(n, e):
                square(n, 0)
                square(n, 1)
                round_hT(e, 0, acc)
                round_hT(e, 1, acc)

            act.dma_start(consts[:], consts_in).then_inc(consts_landed, 16)
            act.dma_start(small[:], bass.AP(smalls.tensor, 0, [[0, P], [1, S_END]])).then_inc(consts_landed, 16)
            act.dma_start(wf_raw[:], wf_in).then_inc(consts_landed, 16)
            act.dma_start(conv_sb[:], conv).then_inc(consts_landed, 16)
            square(0, 0)
            square(0, 1)
            for u in range(RING):
                split_hi(u, u, 1, first=True)
            round_hT(0, 0, acc)
            round_hT(0, 1, acc)
            act.wait_ge(consts_landed, 64)
            nc.scalar.activation(wf_hi[:], wf_raw[:], ACT.Copy).then_inc(setup_act, 1)
            nc.scalar.activation(nsink[:], sink, ACT.Copy, scale=-1.0).then_inc(setup_act, 1)

            for L in range(DEPTH):
                m = MIXER[L]
                item0, v0 = FIRST_ITEM[L], FIRST_V[L]
                if m == FOX:
                    act.wait_ge(sel_landed, 16 * (L // 3 + 1))
                    nc.scalar.activation(sel[:], sel_raw[:], ACT.Copy).then_inc(sel_ready, 1)

                def square_items(cb):
                    for t in range(TT):
                        n = item0 + 2 * cb + t
                        if n >= 2:
                            act.wait_ge(qn_raw, n - 1)
                        width = P if m == SWA and cb == 2 else 512
                        nc.scalar.activation(sq[:, n % 2, 0:width], acc[2 * (cb % 2) + t][:, 0:width],
                                             ACT.Square, scale=HD ** -0.5).then_inc(sq_ready, 1)

                def copy_items(cb):
                    for t in range(TT):
                        n = item0 + 2 * cb + t
                        act.wait_ge(qk_tr, n + 1)
                        dst, c, k = (qT, cb, 4) if cb < 2 else (kT, cb - 2, 4)
                        if m == SWA and cb == 2:
                            k = 2
                        nc.scalar.activation(dst[:, 4 * c:4 * c + k, t * P:(t + 1) * P],
                                             aux[n % 2][:, 0:k * P].rearrange("p (c s) -> p c s", c=k),
                                             ACT.Copy).then_inc(qkT_ready, 1)

                blocks = 3 if m == SWA else 6
                u = FIRST_IN[L]
                for cb in range(blocks):
                    last = u if (m == SWA and cb == 2) else u + 1
                    act.wait_ge(unit_used, last + 1)
                    if cb < (3 if m == SWA else 4):
                        square_items(cb)
                    if m == SWA and cb == 2:
                        for t in range(TT):
                            nc.scalar.activation(v[:, t, 0:P], acc[t][:, P:2 * P], ACT.Copy).then_inc(v_ready, 1)
                    if cb >= 4:
                        for t in range(TT):
                            nc.scalar.activation(v[:, t, (cb - 4) * 512:(cb - 3) * 512],
                                                 acc[2 * (cb % 2) + t][:, :], ACT.Copy).then_inc(v_ready, 1)
                    while u <= last:
                        split_next(u)
                        u += 1
                    if 1 <= cb < 5:
                        copy_items(cb - 1)
                if m == SWA:
                    copy_items(2)
                if m == FOX:
                    k = L // 3
                    act.wait_ge(f_z, k + 1)
                    own.inc(nc.scalar.activation(fe[:], fz[:], ACT.Abs))
                    own.wait()
                    own.inc(nc.scalar.activation(fe[:], fe[:], ACT.Exp, scale=-1.0))
                    own.wait()
                    nc.scalar.activation(fe[:], fe[:], ACT.Ln, bias=1.0).then_inc(f_ln, 1)
                    act.wait_ge(cum_done, k + 1)
                    nc.scalar.activation(cum_hi[:], aux[3][0:HEADS, 256:512], ACT.Copy).then_inc(cum_hi_ready, 1)

                for h in range(HEADS):
                    g = HEADS * L + h
                    for qb in range(2):
                        c0, c1 = (0, P) if qb == 0 else (P, 3 * P)
                        act.wait_ge(s_min, 2 * g + qb + 1)
                        nc.scalar.activation(sc[:, h % 3, c0:c1], sc[:, h % 3, c0:c1], ACT.Exp,
                                             bias=nmax[:, qb, h:h + 1], scale=-1.0,
                                             accum_out=den[:, qb, h:h + 1]).then_inc(p_ready, 1)
                if m == SWA:
                    act.wait_ge(esink_in, 1)
                    nc.scalar.activation(esink[:], esink[:], ACT.Exp).then_inc(esink_ready, 1)
                round_hT(4 * L + 1, 0, aux)
                round_hT(4 * L + 1, 1, aux)

                for k in range(ROW_UNITS - 1):
                    split_next(FIRST_O[L] + k)
                norm(3 * L + 1, 4 * L + 2)
                split_next(FIRST_O[L] + ROW_UNITS - 1)

                def up_unit(u, slot, turn, k):
                    b = slot % 2
                    act.wait_ge(unit_used, u + 1)
                    c = conv_sb[:, L, k, :]
                    if not isinstance(k, int) or FC * L + k >= 2:
                        act.wait_ge(gT_ready, k + (FC * L - 1))
                    nc.scalar.activation(gate_c[:, b, :], aux[slot][:, 0:SEQ], ACT.Identity,
                                         bias=c[:, 3:4], scale=c[:, 2:3]).then_inc(conv_first, 1)
                    nc.scalar.activation(up_c[:, b, :], aux[slot][:, SEQ:2 * SEQ], ACT.Identity,
                                         bias=c[:, 7:8], scale=c[:, 6:7]).then_inc(conv_first, 1)
                    split_hi(u + RING, slot, turn + 1)
                    act.wait_ge(conv_done, k + (FC * L + 1))
                    nc.scalar.activation(gate_c[:, b, :], gate_c[:, b, :], ACT.Silu).then_inc(silu_done, 1)
                    act.wait_ge(prod_done, k + (FC * L + 1))
                    nc.scalar.activation(gT_hi[:, k, :], gate_c[:, b, :], ACT.Copy).then_inc(gT_hi_ready, 1)

                over_units(act, FIRST_UP[L], FC, up_unit, peel=L == 0)
                act.wait_ge(p_landed, 16 * (L + 1))
                nc.scalar.activation(p_hi[:], p_raw[:], ACT.Copy).then_inc(ps_hi, 1)
                over_units(act, FIRST_DOWN[L], DOWN_UNITS - 1, lambda u, slot, turn, k: split_hi(u + RING, slot, turn + 1))
                norm(3 * L + 2, 4 * L + 3)
                split_next(FIRST_DOWN[L] + DOWN_UNITS - 1)
                split_next(FIRST_PLE[L])
                for k in range(ROW_UNITS - 1):
                    split_next(FIRST_GATE[L] + k)
                for t in range(TT):
                    wait_tile(act, 3 * L + 2, t)
                    for b in range(2):
                        nc.scalar.activation(tok[:, t, b * 512:(b + 1) * 512], acc[2 * t + b][:, :],
                                             ACT.Sigmoid).then_inc(sg_ready, 1)
                if L + 1 < DEPTH:
                    norm(3 * L + 3, 4 * L + 4)
                    split_next(FIRST_GATE[L] + ROW_UNITS - 1)

        @block.vector
        def _(dve):
            own = Chain(dve, dve_own)

            def split_lo(u, slot):
                dve.wait_ge(hi_ready, u + 1)
                nc.vector.tensor_tensor(w_lo[:, slot, :], w_raw[:, slot, :], w_hi[:, slot, :].bitcast(F32),
                                        ALU.subtract).then_inc(lo_ready, 1)

            def split_next(u):
                if u + RING < UNITS:
                    split_lo(u + RING, u % RING)

            def add_tile(n, t):
                wait_tile(dve, n - 1, t)
                for b in range(2):
                    c = slice(b * 512, (b + 1) * 512)
                    last = nc.vector.tensor_tensor(x[:, t, c], x[:, t, c], acc[2 * t + b][:, :], ALU.add)
                    if b == 0:
                        own.inc(last)
                last.then_inc(x_ready, 1)

            def normalise(n, t):
                dve.wait_ge(rstd_ready, 2 * n + t + 1)
                dve.wait_ge(gain_landed[n % 2], 16 * (n // 2 + 1))
                nc.vector.scalar_tensor_tensor(tok[:, t, :], x[:, t, :], rstd[:, t:t + 1], gain[:, n % 2, :],
                                               ALU.mult, ALU.mult).then_inc(tok_ready, 1)

            def rest_hT(e, t, banks):
                for b in range(2):
                    dve.wait_ge(hT_hi_ready, 4 * e + 2 * t + b + 1)
                    part = (slice(None), slice(4 * b, 4 * b + 4), slice(t * P, (t + 1) * P))
                    nc.vector.tensor_tensor(hT_lo[part], banks[2 * t + b][:, :].rearrange("p (c s) -> p c s", c=4),
                                            hT_hi[part].bitcast(F32), ALU.subtract).then_inc(hT_ready, 1)

            def norm(n, e, updated=True):
                if updated:
                    add_tile(n, 0)
                normalise(n, 0)
                if updated:
                    add_tile(n, 1)
                normalise(n, 1)
                rest_hT(e, 0, acc)
                rest_hT(e, 1, acc)

            norm(0, 0, updated=False)
            for u in range(RING):
                split_lo(u, u)
            dve.wait_ge(setup_act, 2)
            nc.vector.tensor_tensor(wf_lo[:], wf_raw[:], wf_hi[:].bitcast(F32), ALU.subtract).then_inc(wf_ready, 1)

            for L in range(DEPTH):
                m = MIXER[L]
                item0 = FIRST_ITEM[L]

                def scale_items(cb):
                    heads = 2 if m == SWA and cb == 2 else 8
                    for t in range(TT):
                        n = item0 + 2 * cb + t
                        dve.wait_ge(sq_ready, n + 1)
                        nc.vector.reduce_sum(hsum[:, n % 2, 0:heads],
                                             sq[:, n % 2, 0:heads * HD].rearrange("p (h d) -> p h d", d=HD),
                                             axis=AX.X).then_inc(hsum_ready, 1)
                    for t in range(TT):
                        n = item0 + 2 * cb + t
                        dve.wait_ge(hrstd_ready, n + 1)
                        if n >= 2:
                            dve.wait_ge(qk_tr, n - 1)
                        if m == SWA and cb == 2:
                            dve.wait_ge(v_ready, FIRST_V[L] + t + 1)
                        nc.vector.tensor_tensor(
                            qn[:, n % 2, 0:heads * HD].rearrange("p (h d) -> p h d", d=HD),
                            acc[2 * (cb % 2) + t][:, 0:heads * HD].rearrange("p (h d) -> p h d", d=HD),
                            hrstd[:, n % 2, 0:heads].unsqueeze(2).to_broadcast([P, heads, HD]),
                            ALU.mult).then_inc(qn_raw, 1)

                u = FIRST_IN[L]
                for cb in range(3 if m == SWA else 6):
                    if cb < (3 if m == SWA else 4):
                        scale_items(cb)
                    for _k in range(1 if m == SWA and cb == 2 else 2):
                        split_next(u)
                        u += 1
                if m == FOX:
                    k = L // 3
                    dve.wait_ge(f_done, k + 1)
                    nc.vector.tensor_tensor(fz[:], aux[3][:, 0:2 * HEADS].rearrange("p (t h) -> p t h", t=2),
                                                    bf[:, k, :].unsqueeze(1).to_broadcast([P, 2, HEADS]), ALU.add).then_inc(f_z, 1)
                    dve.wait_ge(f_ln, k + 1)
                    nc.vector.scalar_tensor_tensor(logf[:], fz[:], 0.0, fe[:], ALU.min, ALU.subtract).then_inc(logf_ready, 1)
                    dve.wait_ge(cum_hi_ready, k + 1)
                    nc.vector.tensor_tensor(cum_lo[:], aux[3][0:HEADS, 256:512], cum_hi[:].bitcast(F32),
                                            ALU.subtract).then_inc(cum_ready, 1)

                def mask_scores(h):
                    g = HEADS * L + h
                    dve.wait_ge(s_done, g + 1)
                    if h >= 3:
                        dve.wait_ge(pt_done, g - 2)
                    for qb in range(2):
                        c0, c1 = (0, P) if qb == 0 else (P, 3 * P)
                        if m == REL:
                            add = rel[:, h, P:2 * P] if qb == 0 else rel[:, h, :]
                        else:
                            add = (maskA if m == FOX else maskC)[:, c0:c1]
                        start = nsink[:, h:h + 1] if m == SWA else 3.0e38
                        nc.vector.tensor_tensor_reduce(out=sc[:, h % 3, c0:c1], in0=aux[h % 2][:, c0:c1], in1=add,
                                                       scale=1.0, scalar=start, op0=ALU.add, op1=ALU.min,
                                                       accum_out=nmax[:, qb, h:h + 1]).then_inc(s_min, 1)

                def copy_pT(h):
                    g = HEADS * L + h
                    dve.wait_ge(pt_done, g + 1)
                    if h >= 2:
                        dve.wait_ge(pv_done, g - 1)
                    nc.vector.tensor_copy(pT[:, h % 2, :], aux[2 + h % 2][:, 0:3 * P]).then_inc(pt_copied, 1)

                if m == REL:
                    dve.wait_ge(rel_ready, 1)
                for h in range(HEADS + 1):
                    if h < HEADS:
                        mask_scores(h)
                    if h >= 1:
                        copy_pT(h - 1)
                dve.wait_ge(p_ready, 2 * HEADS * (L + 1))
                if m == SWA:
                    nc.vector.tensor_tensor(esink[:], nmax[:], nsink[:].unsqueeze(1).to_broadcast([P, 2, HEADS]),
                                            ALU.subtract).then_inc(esink_in, 1)
                    dve.wait_ge(esink_ready, 1)
                    own.inc(nc.vector.tensor_tensor(den[:], den[:], esink[:], ALU.add))
                    own.wait()
                own.inc(nc.vector.reciprocal(den[:], den[:]))
                own.wait()
                dve.wait_ge(pv_done, HEADS * (L + 1))
                for t in range(TT):
                    for half in range(2):
                        last = nc.vector.tensor_tensor(
                            tok[:, t, half * 512:(half + 1) * 512].rearrange("p (h d) -> p h d", d=HD),
                            acc[2 * half + t][:, :].rearrange("p (h d) -> p h d", d=HD),
                            den[:, t, 8 * half:8 * half + 8].unsqueeze(2).to_broadcast([P, 8, HD]), ALU.mult)
                        if half == 0:
                            own.inc(last)
                    last.then_inc(tok_ready, 1)
                rest_hT(4 * L + 1, 0, aux)
                rest_hT(4 * L + 1, 1, aux)

                for k in range(ROW_UNITS - 1):
                    split_next(FIRST_O[L] + k)
                norm(3 * L + 1, 4 * L + 2)
                split_next(FIRST_O[L] + ROW_UNITS - 1)


                def up_unit(u, slot, turn, k):
                    b = slot % 2
                    c = conv_sb[:, L, k, :]
                    dve.wait_ge(conv_first, k * 2 + (2 * FC * L + 2))
                    for tap in (1, 0):
                        lag = 2 - tap
                        for half, buf in ((0, gate_c), (1, up_c)):
                            if tap == 0:
                                dve.wait_ge(conv_tap, k * 2 + (2 * FC * L + half + 1))
                            s = aux[slot][:, half * SEQ:half * SEQ + SEQ - lag]
                            ins = nc.vector.scalar_tensor_tensor(buf[:, b, lag:SEQ], s, c[:, 4 * half + tap:4 * half + tap + 1],
                                                                 buf[:, b, lag:SEQ], ALU.mult, ALU.add)
                            if tap == 1:
                                ins.then_inc(conv_tap, 1)
                    ins.then_inc(conv_done, 1)
                    split_lo(u + RING, slot)

                over_units(dve, FIRST_UP[L], FC, up_unit)
                dve.wait_ge(ps_hi, L + 1)
                nc.vector.tensor_tensor(p_lo[:], p_raw[:], p_hi[:].bitcast(F32), ALU.subtract).then_inc(ps_ready, 1)
                over_units(dve, FIRST_DOWN[L], DOWN_UNITS - 1, lambda u, slot, turn, k: split_lo(u + RING, slot))
                norm(3 * L + 2, 4 * L + 3)
                split_next(FIRST_DOWN[L] + DOWN_UNITS - 1)
                split_next(FIRST_PLE[L])
                for k in range(ROW_UNITS - 1):
                    split_next(FIRST_GATE[L] + k)
                for t in range(TT):
                    for b in range(2):
                        c = slice(b * 512, (b + 1) * 512)
                        dve.wait_ge(sg_ready, 4 * L + 2 * t + b + 1)
                        own.inc(nc.vector.tensor_tensor(tok[:, t, c], tok[:, t, c], aux[2 * t + b][:, :], ALU.mult))
                        own.wait()
                        last = nc.vector.tensor_tensor(x[:, t, c], x[:, t, c], tok[:, t, c], ALU.add)
                        if b == 0:
                            own.inc(last)
                    last.then_inc(x_ready, 1)
                if L + 1 < DEPTH:
                    norm(3 * L + 3, 4 * L + 4, updated=False)
                    split_next(FIRST_GATE[L] + ROW_UNITS - 1)

        @block.gpsimd
        def _(pool):
            own = Chain(pool, pool_own)

            def load_gain(n):
                if n >= 2:
                    pool.wait_ge(tok_ready, 2 * norm_event(n - 2) + 2)
                pool.dma_start(gain[:, n % 2, :], bass.AP(gains.tensor, n * D, [[0, P], [1, D]])).then_inc(gain_landed[n % 2], 16)

            def rsqrt(dst, src, width, done):
                own.inc(nc.gpsimd.tensor_scalar(src, src, EPS, None, ALU.add))
                own.wait()
                nc.gpsimd.tensor_tensor(dst, src, neghalf[:, 0:width], ALU.pow).then_inc(done, 1)

            def norm_rstd(n):
                for t in range(TT):
                    pool.wait_ge(ssq_ready, 2 * n + t + 1)
                    rsqrt(rstd[:, t:t + 1], ssq[:, t:t + 1], 1, rstd_ready)

            own.inc(nc.gpsimd.memset(neghalf[:], -0.5))
            load_gain(0)
            load_gain(1)
            pool.dma_start(sel_raw[:], sel_in).then_inc(sel_landed, 16)
            pool.wait_ge(consts_landed, 64)
            for L in range(DEPTH):
                own.inc(nc.gpsimd.tensor_scalar(hgain[:, L, 0, :], hgain[:, L, 0, :], -(HD ** -0.5), None, ALU.mult))
            own.wait()
            for L in range(DEPTH):
                m = MIXER[L]
                item0 = FIRST_ITEM[L]
                norm_rstd(3 * L)
                load_gain(3 * L + 2)
                if L >= 1:
                    pool.wait_ge(unit_used, FIRST_PLE[L - 1] + 1)
                pool.dma_start(p_raw[:], p_in[L]).then_inc(p_landed, 16)
                if m == FOX and L:
                    pool.dma_start(sel_raw[:], sel_in).then_inc(sel_landed, 16)
                if m == REL:
                    pool.dma_start(rel[:], rel_in).then_inc(rel_landed, 16)
                    pool.wait_ge(rel_landed, 16)
                    own.inc(nc.gpsimd.tensor_scalar(rel[:], rel[:], -1.0, None, ALU.mult))
                    own.wait()
                    nc.gpsimd.tensor_tensor(rel[:, :, SEQ - CHUNK:SEQ], rel[:, :, SEQ - CHUNK:SEQ],
                                            maskB.unsqueeze(1).to_broadcast([P, HEADS, CHUNK]), ALU.add).then_inc(rel_ready, 1)
                for i in range(ITEMS[m]):
                    n = item0 + i
                    t = i % 2
                    heads = 2 if m == SWA and i >= 4 else 8
                    for j in range(n, n + 2 if t == 0 else n):
                        pool.wait_ge(hsum_ready, j + 1)
                        rsqrt(hrstd[:, j % 2, 0:heads], hsum[:, j % 2, 0:heads], heads, hrstd_ready)
                    which = 0 if i < 4 else 1
                    item = qn[:, n % 2, 0:heads * HD].rearrange("p (h d) -> p h d", d=HD)
                    pool.wait_ge(qn_raw, n + 1)
                    scaled = nc.gpsimd.tensor_tensor(item, item, hgain[:, L, which, :].unsqueeze(1).to_broadcast([P, heads, HD]), ALU.mult)
                    if m != SWA:
                        scaled.then_inc(qn_ready, 1)
                        continue
                    own.inc(scaled)
                    own.wait()
                    four = lambda a: a.rearrange("p (h a d) -> p h a d", a=2, d=HD // 2)
                    it4, rc, rs = four(qn[:, n % 2, 0:heads * HD]), four(rope_c[:, 0:heads * HD]), four(rope_s[:, 0:heads * HD])
                    for table, to in ((cos, rc), (sin, rs)):
                        for a in range(2):
                            own.inc(nc.gpsimd.tensor_tensor(to[:, :, a, :], it4[:, :, a, :],
                                                            table[:, t, :].unsqueeze(1).to_broadcast([P, heads, HD // 2]), ALU.mult))
                    own.wait()
                    if which == 0:
                        own.inc(nc.gpsimd.tensor_tensor(it4[:, :, 0, :], rc[:, :, 0, :], rs[:, :, 1, :], ALU.subtract))
                        nc.gpsimd.tensor_tensor(it4[:, :, 1, :], rc[:, :, 1, :], rs[:, :, 0, :], ALU.add).then_inc(qn_ready, 1)
                        pool.wait_ge(qn_ready, n + 1)
                    else:
                        kd = kdup[:, t, :].rearrange("p (h c a d) -> p h c a d", c=2, a=2, d=HD // 2)
                        for c in range(2):
                            own.inc(nc.gpsimd.tensor_tensor(kd[:, :, c, 0, :], rc[:, :, 0, :], rs[:, :, 1, :], ALU.subtract))
                            last = nc.gpsimd.tensor_tensor(kd[:, :, c, 1, :], rc[:, :, 1, :], rs[:, :, 0, :], ALU.add)
                            if c == 0:
                                own.inc(last)
                        last.then_inc(qn_ready, 1)
                        pool.wait_ge(qn_ready, n + 1)
                norm_rstd(3 * L + 1)
                if L + 1 < DEPTH:
                    load_gain(3 * L + 3)

                def up_unit(u, slot, turn, k):
                    b = slot % 2
                    pool.wait_ge(silu_done, k + (FC * L + 1))
                    nc.gpsimd.tensor_tensor(gate_c[:, b, :], gate_c[:, b, :], up_c[:, b, :], ALU.mult).then_inc(prod_done, 1)
                    pool.wait_ge(gT_hi_ready, k + (FC * L + 1))
                    nc.gpsimd.tensor_tensor(gT_lo[:, k, :], gate_c[:, b, :], gT_hi[:, k, :].bitcast(F32), ALU.subtract).then_inc(gT_ready, 1)

                over_units(pool, FIRST_UP[L], FC, up_unit)
                norm_rstd(3 * L + 2)
                if L + 1 < DEPTH:
                    load_gain(3 * L + 4)

        @block.tensor
        def _(pe):
            def three(out_ap, l_hi, l_lo, r_hi, r_lo, start, stop):
                nc.tensor.matmul(out_ap, l_hi, r_hi, start=start, stop=False, skip_group_check=True)
                nc.tensor.matmul(out_ap, l_hi, r_lo, start=False, stop=False, skip_group_check=True)
                return nc.tensor.matmul(out_ap, l_lo, r_hi, start=False, stop=stop, skip_group_check=True)

            def transpose_tok(e, banks):
                for t in range(TT):
                    pe.wait_ge(tok_ready, 2 * e + t + 1)
                    for b in range(2):
                        for c in range(4):
                            k = 4 * b + c
                            last = nc.tensor.transpose(banks[2 * t + b][:, c * P:(c + 1) * P],
                                                       tok[:, t, k * P:(k + 1) * P], ident)
                        last.then_inc(tr_done, 1)

            def rows(first, count, left_hi, left_lo, banks, done, waits=None):
                for k in range(count):
                    u = first + k
                    slot = u % RING
                    pe.wait_ge(lo_ready, u + 1)
                    if waits:
                        waits(k)
                    for t in range(TT):
                        ts = slice(t * P, (t + 1) * P)
                        for j in range(2):
                            c = 2 * k + j
                            for l, ws in ((left_hi, (w_hi, w_lo)), (left_lo, (w_hi,))):
                                for w in ws:
                                    for b in range(2):
                                        col = j * D + b * 512
                                        last = nc.tensor.matmul(
                                            banks[2 * t + b][:, :], l[:, c, ts], w[:, slot, col:col + 512],
                                            start=(c == 0 and l is left_hi and w is w_hi),
                                            stop=(c == 2 * count - 1 and l is left_lo), skip_group_check=True)
                        if k == count - 1 and done and t < TT - 1:
                            last.then_inc(done, 1)
                    last.then_inc(unit_used, 1)

            pe.wait_ge(consts_landed, 64)
            transpose_tok(0, acc)
            for L in range(DEPTH):
                m = MIXER[L]
                item0 = FIRST_ITEM[L]

                def in_block(cb, first):
                    for g in range(2):
                        u = first + g
                        pe.wait_ge(lo_ready, u + 1)
                        for t in range(TT):
                            for c in range(4):
                                k = 4 * g + c
                                ts = slice(t * P, (t + 1) * P)
                                col = slice(c * 512, (c + 1) * 512)
                                last = three(acc[2 * (cb % 2) + t][:, :], hT_hi[:, k, ts], hT_lo[:, k, ts],
                                             w_hi[:, u % RING, col], w_lo[:, u % RING, col], k == 0, k == KC - 1)
                        last.then_inc(unit_used, 1)

                def transpose_items(cb):
                    for t in range(TT):
                        n = item0 + 2 * cb + t
                        pe.wait_ge(qn_ready, n + 1)
                        if n >= 2:
                            pe.wait_ge(qkT_ready, n - 1)
                        doubled = m == SWA and cb == 2
                        for c in range(2 if doubled else 4):
                            src = kdup[:, t, c * P:(c + 1) * P] if doubled else qn[:, n % 2, c * P:(c + 1) * P]
                            last = nc.tensor.transpose(aux[n % 2][:, c * P:(c + 1) * P], src, ident)
                        last.then_inc(qk_tr, 1)

                pe.wait_ge(hT_ready, 4 * (4 * L) + 4)
                blocks = 3 if m == SWA else 6
                for cb in range(blocks):
                    if cb >= 2:
                        pe.wait_ge(qn_raw, item0 + 2 * (cb - 1))
                    if m == SWA and cb == 2:
                        u = FIRST_IN[L] + 4
                        pe.wait_ge(lo_ready, u + 1)
                        for t in range(TT):
                            for k in range(KC):
                                ts = slice(t * P, (t + 1) * P)
                                col = slice(k * 256, (k + 1) * 256)
                                last = three(acc[t][:, 0:256], hT_hi[:, k, ts], hT_lo[:, k, ts],
                                             w_hi[:, u % RING, col], w_lo[:, u % RING, col], k == 0, k == KC - 1)
                        last.then_inc(unit_used, 1)
                    else:
                        in_block(cb, FIRST_IN[L] + 2 * cb)
                    if 1 <= cb < 5:
                        transpose_items(cb - 1)
                    if m == FOX and cb == 4:
                        k3 = L // 3
                        pe.wait_ge(wf_ready, 1)
                        for t in range(TT):
                            for k in range(KC):
                                ts = slice(t * P, (t + 1) * P)
                                last = three(aux[3][:, t * HEADS:(t + 1) * HEADS], hT_hi[:, k, ts], hT_lo[:, k, ts],
                                             wf_hi[:, k3, k, :], wf_lo[:, k3, k, :], k == 0, k == KC - 1)
                        last.then_inc(f_done, 1)
                if m == SWA:
                    transpose_items(2)
                if m == FOX:
                    pe.wait_ge(logf_ready, L // 3 + 1)
                    for t in range(TT):
                        last = nc.tensor.matmul(aux[3][0:HEADS, 256:512], logf[:, t, :], tri[:, t, :],
                                                start=(t == 0), stop=(t == TT - 1))
                    last.then_inc(cum_done, 1)
                    pe.wait_ge(sel_ready, L // 3 + 1)
                    pe.wait_ge(cum_ready, L // 3 + 1)
                pe.wait_ge(qkT_ready, item0 + ITEMS[m])
                pe.wait_ge(v_ready, FIRST_V[L] + VS[m])

                def scores(h):
                    g = HEADS * L + h
                    if h >= 2:
                        pe.wait_ge(s_min, 2 * (g - 1))
                    r = slice((h % 2) * HD, (h % 2) * HD + HD)
                    kp = h // 8 if m == SWA else h // 2
                    for qb in range(2):
                        keys = P * (qb + 1)
                        c0 = qb * P
                        dst = aux[h % 2][:, c0:c0 + keys]
                        last = nc.tensor.matmul(dst, qT[r, h // 2, qb * P:(qb + 1) * P], kT[r, kp, 0:keys],
                                                start=True, stop=(m != FOX), skip_group_check=True)
                        if m == FOX:
                            nc.tensor.matmul(dst, sel[:, h, :], cum_hi[:, 0:keys], start=False, stop=False, skip_group_check=True)
                            last = nc.tensor.matmul(dst, sel[:, h, :], cum_lo[:, 0:keys], start=False, stop=True, skip_group_check=True)
                    last.then_inc(s_done, 1)

                def transpose_p(h):
                    g = HEADS * L + h
                    pe.wait_ge(p_ready, 2 * g + 2)
                    if h >= 2:
                        pe.wait_ge(pt_copied, g - 1)
                    for c in range(3):
                        last = nc.tensor.transpose(aux[2 + h % 2][:, c * P:(c + 1) * P], sc[:, h % 3, c * P:(c + 1) * P], ident)
                    last.then_inc(pt_done, 1)

                def values(h):
                    g = HEADS * L + h
                    pe.wait_ge(pt_copied, g + 1)
                    half, o = h // 8, (h % 8) * HD
                    vc = (h // 8 if m == SWA else h) * HD
                    nc.tensor.matmul(acc[2 * half][:, o:o + HD], pT[:, h % 2, 0:P], v[:, 0, vc:vc + HD], start=True, stop=True)
                    nc.tensor.matmul(acc[2 * half + 1][:, o:o + HD], pT[:, h % 2, P:2 * P], v[:, 0, vc:vc + HD], start=True, stop=False)
                    nc.tensor.matmul(acc[2 * half + 1][:, o:o + HD], pT[:, h % 2, 2 * P:3 * P], v[:, 1, vc:vc + HD],
                                     start=False, stop=True).then_inc(pv_done, 1)

                for h in range(HEADS + 2):
                    if h < HEADS:
                        scores(h)
                    if 1 <= h < HEADS + 1:
                        transpose_p(h - 1)
                    if h >= 2:
                        values(h - 2)

                transpose_tok(4 * L + 1, aux)
                pe.wait_ge(hT_ready, 4 * (4 * L + 1) + 4)
                rows(FIRST_O[L], ROW_UNITS, hT_hi, hT_lo, acc, tile_done)

                transpose_tok(4 * L + 2, acc)
                pe.wait_ge(hT_ready, 4 * (4 * L + 2) + 4)

                def up_unit(u, slot, turn, k):
                    pe.wait_ge(lo_ready, u + 1)
                    if not isinstance(k, int) or FC * L + k >= RING:
                        pe.wait_ge(conv_done, k + (FC * L + 1 - RING))
                    for half in range(2):
                        for c in range(KC):
                            col = slice(c * 256 + half * P, c * 256 + (half + 1) * P)
                            dst = aux[slot][:, half * SEQ:(half + 1) * SEQ]
                            nc.tensor.matmul(dst, w_hi[:, slot, col], hT_hi[:, c, :], start=(c == 0), stop=False)
                            nc.tensor.matmul(dst, w_hi[:, slot, col], hT_lo[:, c, :], start=False, stop=False)
                            last = nc.tensor.matmul(dst, w_lo[:, slot, col], hT_hi[:, c, :], start=False, stop=(c == KC - 1))
                    last.then_inc(unit_used, 1)

                over_units(pe, FIRST_UP[L], FC, up_unit, peel=L == 0)
                rows(FIRST_DOWN[L], DOWN_UNITS, gT_hi, gT_lo, acc, tile_done,
                     waits=lambda k: pe.wait_ge(gT_ready, FC * L + 2 * k + 2))
                pe.wait_ge(ps_ready, L + 1)
                rows(FIRST_PLE[L], 1, p_hi, p_lo, aux, None)
                transpose_tok(4 * L + 3, acc)
                pe.wait_ge(hT_ready, 4 * (4 * L + 3) + 4)
                rows(FIRST_GATE[L], ROW_UNITS, hT_hi, hT_lo, acc, tile_done)
                if L + 1 < DEPTH:
                    transpose_tok(4 * L + 4, acc)


def in_units(w):
    w = w.reshape(KC, P, w.shape[1])
    out = []
    for c in range(0, w.shape[2] - 511, 512):
        for g in range(2):
            out.append(w[4 * g:4 * g + 4, :, c:c + 512].transpose(1, 0, 2).reshape(P, UNIT))
    if w.shape[2] % 512:
        out.append(w[:, :, -256:].transpose(1, 0, 2).reshape(P, UNIT))
    return out


def row_units(w):
    w = w.reshape(w.shape[0] // (2 * P), 2, P, D)
    return [a.transpose(1, 0, 2).reshape(P, UNIT) for a in w]


def up_units(w):
    w = w.reshape(KC, P, 2, FC, P)
    return [w[:, :, :, j].transpose(1, 0, 2, 3).reshape(P, UNIT) for j in range(FC)]


def constants():
    t, s = np.arange(P)[:, None], np.arange(SEQ)[None, :]
    c = np.zeros((P, C_END), np.float32)
    c[:, C_ID:C_ID + P] = np.eye(P)
    both = np.concatenate([np.where(s[:, :P] > t, BIG, 0.0), np.where(s > t + P, BIG, 0.0)], 1)
    c[:, C_MASKA:C_MASKC] = both
    seen = lambda q, k: (k // CHUNK <= q // CHUNK) & (k // CHUNK >= q // CHUNK - 1)
    c[:, C_MASKC:C_MASKB] = np.where(np.concatenate([seen(t, s[:, :P]), seen(t + P, s)], 1), 0.0, BIG)
    c[:CHUNK, C_MASKB:C_TRI] = BIG
    c[:, C_TRI:C_COS] = np.concatenate([s >= t, s >= t + P], 1)
    half = HD // 2
    inv = np.float32(10000.0) ** (-np.arange(half, dtype=np.float32) / np.float32(half))
    ang = np.arange(SEQ, dtype=np.float32)[:, None] * inv[None, :]
    tiles = lambda a: a.reshape(TT, P, half).transpose(1, 0, 2).reshape(P, TT * half)
    c[:, C_COS:C_SIN], c[:, C_SIN:C_END] = tiles(np.cos(ang)), tiles(np.sin(ang))
    return c


def kernel(**inputs):
    import concourse.bacc as bacc
    from concourse.bass_utils import run_bass_kernel_spmd

    a = {k: np.asarray(val) for k, val in inputs.items()}
    units = []
    for L, m in enumerate(MIXER):
        w_in = a["w_in_" + "abc"[m]][L // 3]
        w_in = w_in[:, :3 * D] if m == FOX else w_in
        units += in_units(w_in) + row_units(a["w_o"][L]) + up_units(a["w_up"][L])
        units += row_units(a["w_down"][L]) + row_units(a["w_ple_proj"][L]) + row_units(a["w_ple_gate"][L])
    heads = [np.stack([a[f"qn_{'abc'[m]}"][L // 3], a[f"kn_{'abc'[m]}"][L // 3]]) for L, m in enumerate(MIXER)]
    taps = np.concatenate([a["conv_w"], a["conv_b"][:, None]], 1)
    taps = taps.reshape(DEPTH, 4, 2, FC, P).transpose(4, 0, 3, 2, 1).reshape(P, DEPTH, FC, 8)
    dist = np.clip(P + np.arange(P)[:, None] - np.arange(SEQ)[None, :], -P, P) + P
    select = np.zeros((HEADS, HEADS, P), np.float32)
    select[np.arange(HEADS), np.arange(HEADS)] = 1.0
    arrays = {
        "weights": np.stack(units),
        "x_in": a["x"][0],
        "p_in": a["p"][:, 0].reshape(DEPTH, SEQ, 2, P).transpose(0, 3, 2, 1),
        "gains": np.stack([a[k][L] for L in range(DEPTH) for k in ("attn_norm", "ffn_norm", "ple_norm")]),
        "smalls": np.concatenate([np.stack(heads).ravel(), a["b_f"].ravel(), a["sinks"].ravel()]),
        "conv": taps,
        "wf_in": a["w_in_a"][:, :, 3 * D:].reshape(2, KC, P, HEADS).transpose(2, 0, 1, 3),
        "rel_in": a["rel_bias"][0][dist].transpose(0, 2, 1),
        "sel_in": select,
        "consts_in": constants(),
    }
    nc = bacc.Bacc("TRN2", target_bir_lowering=False, num_devices=1)
    arrays = {k: np.ascontiguousarray(val) for k, val in arrays.items()}
    args = {k: nc.dram_tensor(k, val.shape, F32, kind="ExternalInput").ap() for k, val in arrays.items()}
    out = nc.dram_tensor("out", (SEQ, D), F32, kind="ExternalOutput").ap()
    trunk(nc, out=out, **args)
    r = run_bass_kernel_spmd(nc, [arrays], core_ids=[0])
    return r.results[0]["out"].reshape(1, SEQ, D)
```

```python
from contextlib import ExitStack

import concourse.bass as bass
from concourse import mybir
import numpy as np

F32 = mybir.dt.float32
F32R = mybir.dt.float32r
ALU = mybir.AluOpType
ACT = mybir.ActivationFunctionType
AX = mybir.AxisListType

P = 128
D = 1024
SEQ = 256
DEPTH = 4
TT = SEQ // P
KC = D // P
HEADS = 16
HD = 64
D_FF = 2816
FC = D_FF // P
PLE = 256
EPS = 1e-6
CHUNK = 64
BIG = 1.0e30
FOX, REL, SWA = 0, 1, 2
MIXER = [i % 3 for i in range(DEPTH)]

UNIT = 2048
HALF = UNIT // 2
RING = 4
RAW = 4
IN_UNITS = {FOX: 12, REL: 12, SWA: 5}
ROW_UNITS = 4
DOWN_UNITS = FC // 2
DOWN_TAIL = 3

FIRST_IN, FIRST_O, FIRST_PLE, FIRST_UP, FIRST_DOWN, FIRST_GATE = [], [], [], [], [], []
_u = 0
for _m in MIXER:
    FIRST_IN.append(_u)
    FIRST_O.append(_u + IN_UNITS[_m])
    FIRST_PLE.append(FIRST_O[-1] + ROW_UNITS)
    FIRST_UP.append(FIRST_PLE[-1] + 1)
    FIRST_DOWN.append(FIRST_UP[-1] + FC)
    FIRST_GATE.append(FIRST_DOWN[-1] + DOWN_UNITS)
    _u = FIRST_GATE[-1] + ROW_UNITS
UNITS = _u

BLOCKS = {
    FOX: [("q", 0, 2), ("q", 1, 2), ("k", 0, 2), ("k", 1, 2), ("v", 0, 2), ("v", 1, 2)],
    REL: [("q", 0, 2), ("q", 1, 2), ("k", 0, 2), ("k", 1, 2), ("v", 0, 2), ("v", 1, 2)],
    SWA: [("kv", 0, 1), ("q", 0, 2), ("q", 1, 2)],
}
SEQUENCE = {m: [(0, 0), (1, 0), (0, 1), (1, 1)] + [(i, t) for i in range(2, len(b)) for t in range(TT)]
            for m, b in BLOCKS.items()}
FIRST_BLOCK = [sum(len(BLOCKS[m]) for m in MIXER[:i]) for i in range(DEPTH)]
ITEMS = {m: [s for s in SEQUENCE[m] if b[s[0]][0] != "v"] for m, b in BLOCKS.items()}
VS = {m: [s for s in SEQUENCE[m] if "v" in b[s[0]][0]] for m, b in BLOCKS.items()}
FIRST_ITEM = [sum(len(ITEMS[m]) for m in MIXER[:i]) for i in range(DEPTH)]
FIRST_V = [sum(len(VS[m]) for m in MIXER[:i]) for i in range(DEPTH)]

C_MASKA, C_MASKC, C_MASKB, C_SEL, C_COS, C_SIN, C_END = np.cumsum([0, 384, 384, 64, HEADS, 64, 64]).tolist()
S_GAIN, S_SINK, S_END = np.cumsum([0, DEPTH * 2 * HD, HEADS]).tolist()
CUM_LO = 32


LATE = (4, 6, 8, 10)
LAST_UNIT = [u for L in range(DEPTH) for u in (FIRST_PLE[L] - 1, FIRST_GATE[L] - 1, FIRST_GATE[L] + ROW_UNITS - 1)]


def item_heads(m, block):
    return 2 if BLOCKS[m][block][0] == "kv" else 8


class Chain:

    def __init__(self, engine, sem):
        self.engine, self.sem, self.n = engine, sem, 0

    def inc(self, ins):
        ins.then_inc(self.sem, 1)
        self.n += 1

    def wait(self):
        self.engine.wait_ge(self.sem, self.n)


def over_units(engine, first, count, body, peel=False):
    turns = count // RING

    def call(j, i):
        u = first + j
        half = lambda q: ((2 * u + q) % RAW, (2 * u + q) // RAW + 1 + (0 if i is None else i * (2 * RING // RAW)))
        body(u if i is None else i * RING + u, u % RING, half, j if i is None else i * RING + j)

    for j in range(RING if peel else 0):
        call(j, None)
    with engine.Fori(int(peel), turns) as i:
        for j in range(RING):
            call(j, i)
    for j in range(turns * RING, count):
        call(j, None)


def half_of(u):
    return lambda q: ((2 * u + q) % RAW, (2 * u + q) // RAW + 1)


def trunk(nc, weights, x_in, p_in, gains, smalls, bf_in, conv, wf_in, rel_in, ident_in, consts_in, out):
    with ExitStack() as ctx:
        sb = lambda name, shape, dt=F32, c=ctx: c.enter_context(nc.sbuf_tensor(name, shape, dt))
        sem = lambda name: ctx.enter_context(nc.semaphore(name))

        w_raw = sb("w_raw", [P, RAW, HALF])
        w_hi = sb("w_hi", [P, RING, UNIT], F32R)
        w_lo = sb("w_lo", [P, RING, UNIT], F32R)
        x = sb("x", [P, TT, D])
        tok = sb("tok", [P, TT, D])
        hT_hi = sb("hT_hi", [P, KC, SEQ], F32R)
        hT_lo = sb("hT_lo", [P, KC, SEQ], F32R)
        gain = sb("gain", [P, 2, D])
        ident = sb("ident", [P, P])
        consts = sb("consts", [P, C_END])
        small = sb("small", [P, S_END])
        nsink = sb("nsink", [P, HEADS])
        conv_sb = sb("conv_sb", [P, DEPTH, FC, 8])
        wf_raw = sb("wf_raw", [P, 2, KC, HEADS])
        wf_hi = sb("wf_hi", [P, 2, KC, HEADS], F32R)
        wf_lo = sb("wf_lo", [P, 2, KC, HEADS], F32R)
        p_hi = sb("p_hi", [P, 2, SEQ], F32R)
        p_lo = sb("p_lo", [P, 2, SEQ], F32R)
        ssq = sb("ssq", [P, TT])
        rstd = sb("rstd", [P, TT])
        hsum = sb("hsum", [P, 2, 8])
        hrstd = sb("hrstd", [P, 2, 8])
        neghalf = sb("neghalf", [P, 8])
        nmax = sb("nmax", [P, 2, HEADS])
        den = sb("den", [P, 2, HEADS])
        esink = sb("esink", [P, 2, HEADS])
        bf = sb("bf", [HEADS, 2])
        sel = sb("sel", [P, HEADS], F32R)
        cum = sb("cum", [P, SEQ], F32R)
        with ExitStack() as ffn:
            gT_hi = sb("gT_hi", [P, FC, SEQ], F32R, ffn)
            gT_lo = sb("gT_lo", [P, FC, SEQ], F32R, ffn)
            gate_c = sb("gate_c", [P, 2, SEQ], F32, ffn)
            up_c = sb("up_c", [P, 2, SEQ], F32, ffn)
            pp = sb("pp", [P, TT, D], F32, ffn)
        with ExitStack() as early:
            p_raw = sb("p_raw", [P, 2, SEQ], F32, early)
        qT_hi = sb("qT_hi", [P, HEADS // 2, SEQ], F32R)
        qT_lo = sb("qT_lo", [P, HEADS // 2, SEQ], F32R)
        kT_hi = sb("kT_hi", [P, HEADS // 2, SEQ], F32R)
        kT_lo = sb("kT_lo", [P, HEADS // 2, SEQ], F32R)
        v_hi = sb("v_hi", [P, TT, D], F32R)
        v_lo = sb("v_lo", [P, TT, D], F32R)
        pT_hi = sb("pT_hi", [P, 2, 2 * SEQ], F32R)
        pT_lo = sb("pT_lo", [P, 2, 2 * SEQ], F32R)
        with ExitStack() as only_fox:
            fz = sb("fz", [HEADS, SEQ], F32, only_fox)
            fe = sb("fe", [HEADS, SEQ], F32, only_fox)
            fmin = sb("fmin", [HEADS, SEQ], F32, only_fox)
        with ExitStack() as only_swa:
            rope_c = sb("rope_c", [P, 512], F32, only_swa)
            rope_s = sb("rope_s", [P, 512], F32, only_swa)
            kdup = sb("kdup", [P, 2, 256], F32, only_swa)
            rtab = sb("rtab", [P, 2, 2, TT, HD], F32, only_swa)
        with ExitStack() as only_rel:
            rel = sb("rel", [P, 2, 4, SEQ], F32, only_rel)
        sq = tok[:, 0, :].rearrange("p (b n) -> p b n", b=2)
        qn = tok[:, 1, :].rearrange("p (b n) -> p b n", b=2)
        SC = 4
        sc = tok[:].rearrange("p t d -> p (t d)")[:, 0:SC * 3 * P].rearrange("p (b n) -> p b n", b=SC)

        bank = [ctx.enter_context(nc.psum_tensor(f"bank{i}", [P, 512], F32)) for i in range(8)]
        acc, aux = bank[:4], bank[4:]

        maskA = consts[:, C_MASKA:C_MASKA + 384]
        maskC = consts[:, C_MASKC:C_MASKC + 384]
        maskB = consts[:, C_MASKB:C_MASKB + CHUNK]
        sel_raw = consts[:, C_SEL:C_SEL + HEADS]
        cos = consts[:, C_COS:C_COS + 64].rearrange("p (t s) -> p t s", t=TT)
        sin = consts[:, C_SIN:C_SIN + 64].rearrange("p (t s) -> p t s", t=TT)
        hgain = small[:, S_GAIN:S_SINK].rearrange("p (l a d) -> p l a d", l=DEPTH, a=2)
        sink = small[:, S_SINK:S_END]

        raw_landed = [sem(f"raw_landed{i}") for i in range(RAW)]
        hi_ready = sem("hi_ready")
        lo_ready = sem("lo_ready")
        unit_used = sem("unit_used")
        ident_landed = sem("ident_landed")
        consts_landed = sem("consts_landed")
        small_landed = sem("small_landed")
        x_landed = [sem("x_landed0"), sem("x_landed1")]
        gain_first = sem("gain_first")
        gain_landed = [sem("gain_landed0"), sem("gain_landed1")]
        p_landed = sem("p_landed")
        rel_landed = [sem("rel_landed0"), sem("rel_landed1")]
        stored = [sem("stored0"), sem("stored1")]
        sink_ready = sem("sink_ready")
        wf_hi_ready = sem("wf_hi_ready")
        wf_ready = sem("wf_ready")
        zero_ready = sem("zero_ready")
        x_ready = sem("x_ready")
        ssq_ready = sem("ssq_ready")
        rstd_ready = sem("rstd_ready")
        tok_ready = sem("tok_ready")
        tr_done = sem("tr_done")
        hT_hi_ready = sem("hT_hi_ready")
        hT_ready = sem("hT_ready")
        tile_done = sem("tile_done")
        in_done = sem("in_done")
        sq_ready = sem("sq_ready")
        hsum_ready = sem("hsum_ready")
        hrstd_ready = sem("hrstd_ready")
        qn_raw = sem("qn_raw")
        qn_ready = sem("qn_ready")
        qk_tr = sem("qk_tr")
        qkT_hi_ready = sem("qkT_hi_ready")
        qkT_ready = sem("qkT_ready")
        v_hi_ready = sem("v_hi_ready")
        v_ready = sem("v_ready")
        rel_free = sem("rel_free")
        sel_ready = sem("sel_ready")
        f_done = sem("f_done")
        f_z = sem("f_z")
        f_ln = sem("f_ln")
        cum_sum = sem("cum_sum")
        cum_hi_ready = sem("cum_hi_ready")
        cum_zero = sem("cum_zero")
        cum_ready = sem("cum_ready")
        s_done = sem("s_done")
        s_min = sem("s_min")
        p_ready = sem("p_ready")
        rden_ready = sem("rden_ready")
        pn_first = sem("pn_first")
        pn_second = sem("pn_second")
        pt_done = sem("pt_done")
        pt_hi_ready = sem("pt_hi_ready")
        pt_ready = sem("pt_ready")
        pv_done = sem("pv_done")
        o_hi_ready = sem("o_hi_ready")
        o_ready = sem("o_ready")
        esink_ready = sem("esink_ready")
        conv_first = sem("conv_first")
        conv_tap = sem("conv_tap")
        conv_done = sem("conv_done")
        silu_done = sem("silu_done")
        prod_done = sem("prod_done")
        gT_hi_ready = sem("gT_hi_ready")
        gT_ready = sem("gT_ready")
        ps_hi = sem("ps_hi")
        ps_ready = sem("ps_ready")
        pp_first = sem("pp_first")
        pp_second = sem("pp_second")
        sg_ready = sem("sg_ready")
        dve_own = sem("dve_own")
        act_own = sem("act_own")
        pool_own = sem("pool_own")

        def wait_tile(engine, update, t):
            if t == 0:
                engine.wait_ge(tile_done, update + 1)
            else:
                engine.wait_ge(unit_used, LAST_UNIT[update] + 1)

        def wait_block(engine, L, i, t):
            if t == 0:
                engine.wait_ge(in_done, FIRST_BLOCK[L] + i + 1)
            else:
                engine.wait_ge(unit_used, FIRST_IN[L] + sum(b[2] for b in BLOCKS[MIXER[L]][:i + 1]))

        def group(L, name):
            return {"o": range(FIRST_O[L], FIRST_O[L] + ROW_UNITS),
                    "down": range(FIRST_GATE[L] - DOWN_TAIL, FIRST_GATE[L]),
                    "gate": range(FIRST_GATE[L], FIRST_GATE[L] + ROW_UNITS)}[name]

        def item_cols(m, n):
            return item_heads(m, ITEMS[m][n][0]) * HD

        def item_place(m, n):
            kind, c, _ = BLOCKS[m][ITEMS[m][n][0]]
            return ((qT_hi, qT_lo) if kind == "q" else (kT_hi, kT_lo)) + (4 * c, 2 if kind == "kv" else 4)

        block = ctx.enter_context(nc.Block())

        @block.sync
        def _(sp):
            for t in range(TT):
                sp.dma_start(x[:, t, :], x_in[t * P:(t + 1) * P, :]).then_inc(x_landed[t], 16)
                if t == 0:
                    sp.dma_start(ident[:], ident_in).then_inc(ident_landed, 16)
                    sp.dma_start(gain[:, 0, :], bass.AP(gains.tensor, 0, [[0, P], [1, D]])).then_inc(gain_first, 16)
                for g in range(t * 2, t * 2 + 2):
                    sp.dma_start(w_raw[:, g, :], weights[g]).then_inc(raw_landed[g], 16)
            turns = 2 * UNITS // RAW
            with sp.Fori(1, turns) as i:
                for j in range(RAW):
                    sp.wait_ge(lo_ready, i * RAW + (j - RAW + 1))
                    sp.dma_start(w_raw[:, j, :], weights[i * RAW + j]).then_inc(raw_landed[j], 16)
            for g in range(turns * RAW, 2 * UNITS):
                sp.wait_ge(lo_ready, g - RAW + 1)
                sp.dma_start(w_raw[:, g % RAW, :], weights[g]).then_inc(raw_landed[g % RAW], 16)
            for t in range(TT):
                sp.wait_ge(x_ready, 2 * (3 * DEPTH - 1) + t + 1)
                sp.dma_start(out[t * P:(t + 1) * P, :], x[:, t, :]).then_inc(stored[t], 16)
            for t in range(TT):
                sp.wait_ge(stored[t], 16)

        @block.scalar
        def _(act):
            own = Chain(act, act_own)

            def split_hi(u, slot, half, first=False, halves=(0, 1)):
                for q in halves:
                    raw, loads = half(q)
                    act.wait_ge(raw_landed[raw], loads * 16)
                    if not first and q == 0:
                        act.wait_ge(unit_used, u - (RING - 1))
                    nc.scalar.activation(w_hi[:, slot, q * HALF:(q + 1) * HALF], w_raw[:, raw, :], ACT.Copy).then_inc(hi_ready, 1)

            def split_next(u):
                if u + RING < UNITS:
                    split_hi(u + RING, u % RING, half_of(u + RING))

            def split_late_hi(L, j):
                u = FIRST_O[L] - 2 + j // 2 + RING
                split_hi(u, u % RING, half_of(u), halves=(j % 2,))

            def split_looped(u, slot, half, k):
                split_hi(u + RING, slot, lambda q: (half(q)[0], half(q)[1] + 2 * RING // RAW))

            def square(n, t):
                if n == 0:
                    act.wait_ge(x_landed[t], 16)
                else:
                    act.wait_ge(x_ready, 2 * (n - 1) + t + 1)
                nc.scalar.activation(tok[:, t, :], x[:, t, :], ACT.Square, scale=D ** -0.5,
                                     accum_out=ssq[:, t:t + 1]).then_inc(ssq_ready, 1)

            def round_hT(n, t):
                for b in range(2):
                    act.wait_ge(tr_done, 4 * n + 2 * t + b + 1)
                    nc.scalar.activation(hT_hi[:, 4 * b:4 * b + 4, t * P:(t + 1) * P],
                                         acc[2 * t + b][:, :].rearrange("p (c s) -> p c s", c=4),
                                         ACT.Copy).then_inc(hT_hi_ready, 1)

            def sigmoids(L, t):
                wait_tile(act, 3 * L + 2, t)
                for b in range(2):
                    nc.scalar.activation(tok[:, t, b * 512:(b + 1) * 512], acc[2 * t + b][:, :],
                                         ACT.Sigmoid).then_inc(sg_ready, 1)

            def norm(n, units, before=None, between=None):
                units = list(units)
                if before:
                    before(0)
                square(n, 0)
                for u in units[:-2]:
                    split_next(u)
                round_hT(n, 0)
                split_next(units[-2])
                if before:
                    before(1)
                square(n, 1)
                if between:
                    between()
                    round_hT(n, 1)
                    split_next(units[-1])
                else:
                    split_next(units[-1])
                    round_hT(n, 1)

            square(0, 0)
            split_hi(0, 0, half_of(0), first=True)
            round_hT(0, 0)
            square(0, 1)
            split_hi(1, 1, half_of(1), first=True)
            split_hi(2, 2, half_of(2), first=True)
            round_hT(0, 1)
            split_hi(3, 3, half_of(3), first=True)
            act.wait_ge(small_landed, 64)
            nc.scalar.activation(wf_hi[:], wf_raw[:], ACT.Copy).then_inc(wf_hi_ready, 1)
            nc.scalar.activation(nsink[:], sink, ACT.Copy, scale=-1.0).then_inc(sink_ready, 1)
            act.wait_ge(consts_landed, 16)
            nc.scalar.activation(sel[:], sel_raw, ACT.Copy).then_inc(sel_ready, 1)

            for L in range(DEPTH):
                m = MIXER[L]
                item0, v0 = FIRST_ITEM[L], FIRST_V[L]
                act.wait_ge(p_landed, 16 * (L + 1))
                nc.scalar.activation(p_hi[:], p_raw[:], ACT.Copy).then_inc(ps_hi, 1)

                def copy_items(pair):
                    for i in (2 * pair, 2 * pair + 1):
                        n = item0 + i
                        act.wait_ge(qk_tr, n + 1)
                        hi, _, c, k = item_place(m, i)
                        t = ITEMS[m][i][1]
                        nc.scalar.activation(hi[:, c:c + k, t * P:(t + 1) * P],
                                             aux[n % 2][:, 0:k * P].rearrange("p (c s) -> p c s", c=k),
                                             ACT.Copy).then_inc(qkT_hi_ready, 1)

                unit = FIRST_IN[L]
                for s, (i, t) in enumerate(SEQUENCE[m]):
                    kind, c, units = BLOCKS[m][i]
                    src = acc[2 * t + i % 2]
                    wait_block(act, L, i, t)
                    if kind != "v":
                        it = ITEMS[m].index((i, t))
                        n = item0 + it
                        if n >= 2:
                            act.wait_ge(qn_raw, n - 1)
                        nc.scalar.activation(sq[:, n % 2, 0:item_cols(m, it)], src[:, 0:item_cols(m, it)],
                                             ACT.Square, scale=HD ** -0.5).then_inc(sq_ready, 1)
                    if kind == "v":
                        nc.scalar.activation(v_hi[:, t, c * 512:(c + 1) * 512], src[:, :], ACT.Copy).then_inc(v_hi_ready, 1)
                    if kind == "kv":
                        for twice in range(2):
                            ins = nc.scalar.activation(
                                v_hi[:, t, 0:256].rearrange("p (h c d) -> p h c d", c=2, d=HD)[:, :, twice, :],
                                src[:, P:2 * P].rearrange("p (h d) -> p h d", d=HD), ACT.Copy)
                        ins.then_inc(v_hi_ready, 1)
                    if t == 1:
                        if i < len(BLOCKS[m]) - 1:
                            for _ in range(units):
                                split_next(unit)
                                unit += 1
                    if s % 2 and s >= 3 and s - 3 < len(ITEMS[m]):
                        copy_items((s - 3) // 2)
                    if m == FOX and s == 7:
                        act.wait_ge(cum_sum, L // 3 + 1)
                        act.wait_ge(cum_zero, 1)
                        nc.scalar.activation(cum[0:HEADS, :], fz[:], ACT.Copy).then_inc(cum_hi_ready, 1)
                    if m == FOX and s == 4:
                        k = L // 3
                        act.wait_ge(f_z, k + 1)
                        own.inc(nc.scalar.activation(fe[:], fz[:], ACT.Abs))
                        own.wait()
                        own.inc(nc.scalar.activation(fe[:], fe[:], ACT.Exp, scale=-1.0))
                        own.wait()
                        nc.scalar.activation(fe[:], fe[:], ACT.Ln, bias=1.0).then_inc(f_ln, 1)
                if m == SWA:
                    copy_items(2)

                def exps(h):
                    g = HEADS * L + h
                    for qb in range(2):
                        c0, c1 = (0, P) if qb == 0 else (P, 3 * P)
                        act.wait_ge(s_min, 2 * g + qb + 1)
                        nc.scalar.activation(sc[:, h % SC, c0:c1], sc[:, h % SC, c0:c1], ACT.Exp,
                                             bias=nmax[:, qb, h:h + 1], scale=-1.0,
                                             accum_out=den[:, qb, h:h + 1]).then_inc(p_ready, 1)
                    if m == SWA:
                        nc.scalar.activation(esink[:, :, h], nmax[:, :, h], ACT.Exp, bias=sink[:, h:h + 1]).then_inc(esink_ready, 1)

                def round_pT(h):
                    g = HEADS * L + h
                    act.wait_ge(pt_done, g + 1)
                    if h >= 2:
                        act.wait_ge(pv_done, g - 1)
                    nc.scalar.activation(pT_hi[:, h % 2, P:4 * P], aux[2 + h % 2][:, P:4 * P], ACT.Copy).then_inc(pt_hi_ready, 1)

                def round_o(pair):
                    act.wait_ge(pv_done, HEADS * L + 2 * pair + 2)
                    for e in range(2):
                        r = slice(e * HD, (e + 1) * HD)
                        ins = nc.scalar.activation(hT_hi[r, pair, :], acc[2 + pair % 2][r, e * SEQ:(e + 1) * SEQ], ACT.Copy)
                    ins.then_inc(o_hi_ready, 1)

                for h in range(HEADS + 4):
                    if h < HEADS:
                        exps(h)
                    if 2 <= h < HEADS + 2:
                        round_pT(h - 2)
                    if h >= 5 and h % 2:
                        round_o((h - 5) // 2)
                    if h in LATE:
                        split_late_hi(L, LATE.index(h))

                def copy_pp():
                    act.wait_ge(unit_used, FIRST_PLE[L] + 1)
                    for b in range(2):
                        nc.scalar.activation(pp[:, 0, b * 512:(b + 1) * 512], aux[b][:, :], ACT.Copy).then_inc(pp_first, 1)

                norm(3 * L + 1, group(L, "o"), between=copy_pp)
                split_next(FIRST_PLE[L])

                def up_unit(u, slot, half, k):
                    b = slot % 2
                    act.wait_ge(unit_used, u + 1)
                    c = conv_sb[:, L, k, :]
                    if not isinstance(k, int) or FC * L + k >= 2:
                        act.wait_ge(gT_ready, k + (FC * L - 1))
                    nc.scalar.activation(gate_c[:, b, :], aux[slot][:, 0:SEQ], ACT.Identity,
                                         bias=c[:, 3:4], scale=c[:, 2:3]).then_inc(conv_first, 1)
                    nc.scalar.activation(up_c[:, b, :], aux[slot][:, SEQ:2 * SEQ], ACT.Identity,
                                         bias=c[:, 7:8], scale=c[:, 6:7]).then_inc(conv_first, 1)
                    split_looped(u, slot, half, k)
                    act.wait_ge(conv_done, k + (FC * L + 1))
                    nc.scalar.activation(gate_c[:, b, :], gate_c[:, b, :], ACT.Silu).then_inc(silu_done, 1)
                    act.wait_ge(prod_done, k + (FC * L + 1))
                    nc.scalar.activation(gT_hi[:, k, :], gate_c[:, b, :], ACT.Copy).then_inc(gT_hi_ready, 1)

                act.preload_act_table(ACT.Silu)
                over_units(act, FIRST_UP[L], FC, up_unit, peel=L == 0)
                over_units(act, FIRST_DOWN[L], DOWN_UNITS - DOWN_TAIL, split_looped)
                norm(3 * L + 2, group(L, "down"))
                act.preload_act_table(ACT.Sigmoid)
                if L + 1 < DEPTH:
                    norm(3 * L + 3, group(L, "gate"), before=lambda t: sigmoids(L, t))
                else:
                    sigmoids(L, 0)
                    sigmoids(L, 1)

        @block.vector
        def _(dve):
            own = Chain(dve, dve_own)

            def split_lo(u, slot, half, halves=(0, 1)):
                for q in halves:
                    dve.wait_ge(hi_ready, u * 2 + (q + 1))
                    cols = slice(q * HALF, (q + 1) * HALF)
                    nc.vector.tensor_tensor(w_lo[:, slot, cols], w_raw[:, half(q)[0], :], w_hi[:, slot, cols].bitcast(F32),
                                            ALU.subtract).then_inc(lo_ready, 1)

            def split_next(u):
                if u + RING < UNITS:
                    split_lo(u + RING, u % RING, half_of(u + RING))

            def split_late_lo(L, j):
                u = FIRST_O[L] - 2 + j // 2 + RING
                split_lo(u, u % RING, half_of(u), halves=(j % 2,))

            def split_looped(u, slot, half, k):
                split_lo(u + RING, slot, half)

            def add_tile(n, t):
                wait_tile(dve, n - 1, t)
                for b in range(2):
                    c = slice(b * 512, (b + 1) * 512)
                    last = nc.vector.tensor_tensor(x[:, t, c], x[:, t, c], acc[2 * t + b][:, :], ALU.add)
                    if b == 0:
                        own.inc(last)
                last.then_inc(x_ready, 1)

            def add_gated(L, t):
                for b in range(2):
                    c = slice(b * 512, (b + 1) * 512)
                    dve.wait_ge(sg_ready, 4 * L + 2 * t + b + 1)
                    if t == 0 and b == 0:
                        dve.wait_ge(pp_first, 2 * (L + 1))
                        dve.wait_ge(pp_second, 2 * (L + 1))
                    own.inc(nc.vector.tensor_tensor(tok[:, t, c], tok[:, t, c], pp[:, t, c], ALU.mult))
                    own.wait()
                    last = nc.vector.tensor_tensor(x[:, t, c], x[:, t, c], tok[:, t, c], ALU.add)
                    if b == 0:
                        own.inc(last)
                last.then_inc(x_ready, 1)

            def normalise(n, t):
                dve.wait_ge(rstd_ready, 2 * n + t + 1)
                if n == 0:
                    dve.wait_ge(gain_first, 16)
                else:
                    dve.wait_ge(gain_landed[n % 2], 16 * ((n + 1) // 2))
                nc.vector.scalar_tensor_tensor(tok[:, t, :], x[:, t, :], rstd[:, t:t + 1], gain[:, n % 2, :],
                                               ALU.mult, ALU.mult).then_inc(tok_ready, 1)

            def rest_hT(n, t):
                for b in range(2):
                    dve.wait_ge(hT_hi_ready, 4 * n + 2 * t + b + 1)
                    part = (slice(None), slice(4 * b, 4 * b + 4), slice(t * P, (t + 1) * P))
                    nc.vector.tensor_tensor(hT_lo[part], acc[2 * t + b][:, :].rearrange("p (c s) -> p c s", c=4),
                                            hT_hi[part].bitcast(F32), ALU.subtract).then_inc(hT_ready, 1)

            def norm(n, units, add, between=None):
                units = list(units)
                add(0)
                normalise(n, 0)
                for u in units[:-2]:
                    split_next(u)
                rest_hT(n, 0)
                split_next(units[-2])
                add(1)
                normalise(n, 1)
                if between:
                    between()
                    rest_hT(n, 1)
                    split_next(units[-1])
                else:
                    split_next(units[-1])
                    rest_hT(n, 1)

            dve.wait_ge(x_landed[0], 16)
            normalise(0, 0)
            split_lo(0, 0, half_of(0))
            rest_hT(0, 0)
            dve.wait_ge(x_landed[1], 16)
            normalise(0, 1)
            split_lo(1, 1, half_of(1))
            split_lo(2, 2, half_of(2))
            rest_hT(0, 1)
            split_lo(3, 3, half_of(3))
            dve.wait_ge(wf_hi_ready, 1)
            nc.vector.tensor_tensor(wf_lo[:], wf_raw[:], wf_hi[:].bitcast(F32), ALU.subtract).then_inc(wf_ready, 1)

            for L in range(DEPTH):
                m = MIXER[L]
                item0, v0 = FIRST_ITEM[L], FIRST_V[L]
                dve.wait_ge(ps_hi, L + 1)
                nc.vector.tensor_tensor(p_lo[:], p_raw[:], p_hi[:].bitcast(F32), ALU.subtract).then_inc(ps_ready, 1)

                def sum_item(i):
                    n, cols = item0 + i, item_cols(m, i)
                    dve.wait_ge(sq_ready, n + 1)
                    nc.vector.reduce_sum(hsum[:, n % 2, 0:cols // HD],
                                         sq[:, n % 2, 0:cols].rearrange("p (h d) -> p h d", d=HD),
                                         axis=AX.X).then_inc(hsum_ready, 1)

                def scale_item(i):
                    n, cols = item0 + i, item_cols(m, i)
                    blk, t = ITEMS[m][i]
                    dve.wait_ge(hrstd_ready, n + 1)
                    if n >= 2:
                        dve.wait_ge(qk_tr, n - 1)
                    if BLOCKS[m][blk][0] == "kv":
                        dve.wait_ge(v_hi_ready, v0 + VS[m].index((blk, t)) + 1)
                    nc.vector.tensor_tensor(
                        qn[:, n % 2, 0:cols].rearrange("p (h d) -> p h d", d=HD),
                        acc[2 * t + blk % 2][:, 0:cols].rearrange("p (h d) -> p h d", d=HD),
                        hrstd[:, n % 2, 0:cols // HD].unsqueeze(2).to_broadcast([P, cols // HD, HD]),
                        ALU.mult).then_inc(qn_raw, 1)

                def rest_items(pair):
                    for i in (2 * pair, 2 * pair + 1):
                        n = item0 + i
                        dve.wait_ge(qkT_hi_ready, n + 1)
                        hi, lo, c, k = item_place(m, i)
                        t = ITEMS[m][i][1]
                        part = (slice(None), slice(c, c + k), slice(t * P, (t + 1) * P))
                        nc.vector.tensor_tensor(lo[part], aux[n % 2][:, 0:k * P].rearrange("p (c s) -> p c s", c=k),
                                                hi[part].bitcast(F32), ALU.subtract).then_inc(qkT_ready, 1)

                def rest_v(blk, t):
                    kind, c, _ = BLOCKS[m][blk]
                    src = acc[2 * t + blk % 2]
                    dve.wait_ge(v_hi_ready, v0 + VS[m].index((blk, t)) + 1)
                    if kind == "v":
                        cols = slice(c * 512, (c + 1) * 512)
                        ins = nc.vector.tensor_tensor(v_lo[:, t, cols], src[:, :], v_hi[:, t, cols].bitcast(F32), ALU.subtract)
                    else:
                        for twice in range(2):
                            at = lambda a: a[:, t, 0:256].rearrange("p (h c d) -> p h c d", c=2, d=HD)[:, :, twice, :]
                            ins = nc.vector.tensor_tensor(at(v_lo), src[:, P:2 * P].rearrange("p (h d) -> p h d", d=HD),
                                                          at(v_hi).bitcast(F32), ALU.subtract)
                    ins.then_inc(v_ready, 1)

                unit = FIRST_IN[L]
                for s, (blk, t) in enumerate(SEQUENCE[m]):
                    released = []
                    if t == 1 and blk < len(BLOCKS[m]) - 1:
                        released = list(range(unit, unit + BLOCKS[m][blk][2]))
                        unit += len(released)
                    is_item = (blk, t) in ITEMS[m]
                    if is_item:
                        sum_item(s)
                    if released:
                        split_next(released.pop(0))
                    if is_item:
                        scale_item(s)
                    if (blk, t) in VS[m]:
                        rest_v(blk, t)
                    for u in released:
                        split_next(u)
                    if s % 2 and s >= 3 and s - 3 < len(ITEMS[m]):
                        rest_items((s - 3) // 2)
                    if m == FOX and s == 3:
                        k = L // 3
                        dve.wait_ge(f_done, k + 1)
                        nc.vector.tensor_scalar(fz[:], aux[3][0:HEADS, 0:SEQ], bf[:, k:k + 1], None, ALU.add).then_inc(f_z, 1)
                    if m == FOX and s == 5:
                        own.inc(nc.vector.tensor_scalar(fmin[:], fz[:], 0.0, None, ALU.min))
                        own.wait()
                        dve.wait_ge(f_ln, k + 1)
                        nc.vector.tensor_tensor_scan(fz[:], fmin[:], fe[:], 0.0, ALU.add, ALU.subtract).then_inc(cum_sum, 1)
                    if m == FOX and s == 7:
                        dve.wait_ge(cum_hi_ready, k + 1)
                        nc.vector.tensor_tensor(cum[CUM_LO:CUM_LO + HEADS, :], fz[:], cum[0:HEADS, :].bitcast(F32),
                                                ALU.subtract).then_inc(cum_ready, 1)
                if m == SWA:
                    rest_items(2)

                def negate_bias(g4):
                    dve.wait_ge(rel_landed[g4 % 2], 16 * (g4 // 2 + 1))
                    r = rel[:, g4 % 2, :, :]
                    own.inc(nc.vector.tensor_scalar(r, r, -1.0, None, ALU.mult))
                    own.wait()
                    own.inc(nc.vector.tensor_tensor(r[:, :, SEQ - CHUNK:SEQ], r[:, :, SEQ - CHUNK:SEQ],
                                                    maskB.unsqueeze(1).to_broadcast([P, 4, CHUNK]), ALU.add))
                    own.wait()

                def mask_scores(h):
                    g = HEADS * L + h
                    dve.wait_ge(s_done, g + 1)
                    if h >= SC:
                        dve.wait_ge(pt_done, g - SC + 1)
                    for qb in range(2):
                        c0, c1 = (0, P) if qb == 0 else (P, 3 * P)
                        if m == REL:
                            add = rel[:, (h // 4) % 2, h % 4, P * (1 - qb):SEQ]
                        else:
                            add = (maskA if m == FOX else maskC)[:, c0:c1]
                        start = nsink[:, h:h + 1] if m == SWA else 3.0e38
                        nc.vector.tensor_tensor_reduce(out=sc[:, h % SC, c0:c1], in0=aux[h % 2][:, qb * SEQ:qb * SEQ + c1 - c0],
                                                       in1=add, scale=1.0, scalar=start, op0=ALU.add, op1=ALU.min,
                                                       accum_out=nmax[:, qb, h:h + 1]).then_inc(s_min, 1)

                def invert_sums(h):
                    g = HEADS * L + h
                    dve.wait_ge(p_ready, 2 * g + 2)
                    if m == SWA:
                        dve.wait_ge(esink_ready, h + 1)
                        own.inc(nc.vector.tensor_tensor(den[:, :, h], den[:, :, h], esink[:, :, h], ALU.add))
                        own.wait()
                    nc.vector.reciprocal(den[:, :, h], den[:, :, h]).then_inc(rden_ready, 1)
                    dve.wait_ge(rden_ready, g + 1)
                    nc.vector.tensor_scalar(sc[:, h % SC, P:3 * P], sc[:, h % SC, P:3 * P], den[:, 1, h:h + 1], None,
                                            ALU.mult).then_inc(pn_second, 1)

                def rest_pT(h):
                    dve.wait_ge(pt_hi_ready, HEADS * L + h + 1)
                    nc.vector.tensor_tensor(pT_lo[:, h % 2, P:4 * P], aux[2 + h % 2][:, P:4 * P],
                                            pT_hi[:, h % 2, P:4 * P].bitcast(F32), ALU.subtract).then_inc(pt_ready, 1)

                def rest_o(pair):
                    dve.wait_ge(o_hi_ready, HEADS // 2 * L + pair + 1)
                    for e in range(2):
                        r = slice(e * HD, (e + 1) * HD)
                        ins = nc.vector.tensor_tensor(hT_lo[r, pair, :], acc[2 + pair % 2][r, e * SEQ:(e + 1) * SEQ],
                                                      hT_hi[r, pair, :].bitcast(F32), ALU.subtract)
                    ins.then_inc(o_ready, 1)

                if m == SWA:
                    dve.wait_ge(sink_ready, 1)
                if m == REL:
                    negate_bias(0)
                for h in range(HEADS + 4):
                    if h < HEADS:
                        mask_scores(h)
                    if 1 <= h < HEADS + 1:
                        invert_sums(h - 1)
                    if 2 <= h < HEADS + 2:
                        rest_pT(h - 2)
                    if h >= 5 and h % 2:
                        rest_o((h - 5) // 2)
                    if h in LATE:
                        split_late_lo(L, LATE.index(h))
                    if m == REL and h % 4 == 2 and h < HEADS - 2:
                        negate_bias(h // 4 + 1)

                def copy_pp():
                    dve.wait_ge(unit_used, FIRST_PLE[L] + 1)
                    for b in range(2):
                        nc.vector.tensor_copy(pp[:, 1, b * 512:(b + 1) * 512], aux[2 + b][:, :]).then_inc(pp_second, 1)

                norm(3 * L + 1, group(L, "o"), lambda t: add_tile(3 * L + 1, t), between=copy_pp)
                split_next(FIRST_PLE[L])

                def up_unit(u, slot, half, k):
                    b = slot % 2
                    c = conv_sb[:, L, k, :]
                    dve.wait_ge(conv_first, k * 2 + (2 * FC * L + 2))
                    for tap in (1, 0):
                        lag = 2 - tap
                        for side, buf in ((0, gate_c), (1, up_c)):
                            if tap == 0:
                                dve.wait_ge(conv_tap, k * 2 + (2 * FC * L + side + 1))
                            ins = nc.vector.scalar_tensor_tensor(
                                buf[:, b, lag:SEQ], aux[slot][:, side * SEQ:side * SEQ + SEQ - lag],
                                c[:, 4 * side + tap:4 * side + tap + 1], buf[:, b, lag:SEQ], ALU.mult, ALU.add)
                            if tap == 1:
                                ins.then_inc(conv_tap, 1)
                    ins.then_inc(conv_done, 1)
                    split_looped(u, slot, half, k)

                over_units(dve, FIRST_UP[L], FC, up_unit)
                over_units(dve, FIRST_DOWN[L], DOWN_UNITS - DOWN_TAIL, split_looped)
                norm(3 * L + 2, group(L, "down"), lambda t: add_tile(3 * L + 2, t))
                if L + 1 < DEPTH:
                    norm(3 * L + 3, group(L, "gate"), lambda t: add_gated(L, t))
                else:
                    add_gated(L, 0)
                    add_gated(L, 1)

        @block.gpsimd
        def _(pool):
            own = Chain(pool, pool_own)

            def load_gain(n):
                if n >= 2:
                    pool.wait_ge(tok_ready, 2 * (n - 2) + 2)
                pool.dma_start(gain[:, n % 2, :], bass.AP(gains.tensor, n * D, [[0, P], [1, D]])).then_inc(gain_landed[n % 2], 16)

            def load_bias(g4):
                pool.dma_start(rel[:, g4 % 2, :, :], rel_in[:, 4 * g4:4 * g4 + 4, :]).then_inc(rel_landed[g4 % 2], 16)

            def rsqrt(dst, src, width, done):
                own.inc(nc.gpsimd.tensor_scalar(src, src, EPS, None, ALU.add))
                own.wait()
                nc.gpsimd.tensor_tensor(dst, src, neghalf[:, 0:width], ALU.pow).then_inc(done, 1)

            def norm_rstd(n):
                for t in range(TT):
                    pool.wait_ge(ssq_ready, 2 * n + t + 1)
                    rsqrt(rstd[:, t:t + 1], ssq[:, t:t + 1], 1, rstd_ready)

            own.inc(nc.gpsimd.memset(neghalf[:], -0.5))
            own.wait()
            pool.dma_start(small[:], bass.AP(smalls.tensor, 0, [[0, P], [1, S_END]])).then_inc(small_landed, 16)
            norm_rstd(0)
            pool.dma_start(p_raw[:], p_in[0]).then_inc(p_landed, 16)
            pool.dma_start(wf_raw[:], wf_in).then_inc(small_landed, 16)
            pool.dma_start(bf[:], bf_in).then_inc(small_landed, 16)
            pool.dma_start(consts[:], consts_in).then_inc(consts_landed, 16)
            pool.dma_start(conv_sb[:], conv).then_inc(small_landed, 16)
            load_gain(1)
            nc.gpsimd.memset(cum[:].bitcast(F32), 0.0).then_inc(cum_zero, 1)
            pool.wait_ge(small_landed, 64)
            own.inc(nc.gpsimd.tensor_scalar(hgain[:, :, 0, :], hgain[:, :, 0, :], -(HD ** -0.5), None, ALU.mult))
            own.wait()
            for L in range(DEPTH):
                m = MIXER[L]
                item0 = FIRST_ITEM[L]
                if L:
                    pool.wait_ge(unit_used, FIRST_GATE[L - 1])
                    pool.dma_start(p_raw[:], p_in[L]).then_inc(p_landed, 16)
                    pool.wait_ge(unit_used, LAST_UNIT[3 * L - 1])
                    norm_rstd(3 * L)
                load_gain(3 * L + 2)
                if m == REL:
                    load_bias(0)
                    load_bias(1)
                for part in (pT_hi, pT_lo):
                    ins = nc.gpsimd.memset(part[:, :, 0:P].bitcast(F32), 0.0)
                    ins.then_inc(zero_ready, 1)
                if m == SWA:
                    for which in range(2):
                        for table, a in ((cos, 0), (sin, 1)):
                            own.inc(nc.gpsimd.tensor_tensor(
                                rtab[:, which, a, :, :].rearrange("p t (a d) -> p t a d", a=2),
                                table.unsqueeze(2).to_broadcast([P, TT, 2, HD // 2]),
                                hgain[:, L, which, :].rearrange("p (a d) -> p a d", a=2).unsqueeze(1).to_broadcast([P, TT, 2, HD // 2]),
                                ALU.mult))
                    own.wait()
                for i, (blk, t) in enumerate(ITEMS[m]):
                    n = item0 + i
                    kind = BLOCKS[m][blk][0]
                    which = 0 if kind == "q" else 1
                    heads = item_heads(m, blk)
                    pool.wait_ge(hsum_ready, n + 1)
                    rsqrt(hrstd[:, n % 2, 0:heads], hsum[:, n % 2, 0:heads], heads, hrstd_ready)
                    item = qn[:, n % 2, 0:heads * HD].rearrange("p (h d) -> p h d", d=HD)
                    pool.wait_ge(qn_raw, n + 1)
                    if m != SWA:
                        nc.gpsimd.tensor_tensor(item, item, hgain[:, L, which, :].unsqueeze(1).to_broadcast([P, heads, HD]),
                                                ALU.mult).then_inc(qn_ready, 1)
                        continue
                    for a, to in ((0, rope_c), (1, rope_s)):
                        own.inc(nc.gpsimd.tensor_tensor(to[:, 0:heads * HD].rearrange("p (h d) -> p h d", d=HD), item,
                                                        rtab[:, which, a, t, :].unsqueeze(1).to_broadcast([P, heads, HD]), ALU.mult))
                    own.wait()
                    four = lambda a: a.rearrange("p (h a d) -> p h a d", a=2, d=HD // 2)
                    rc, rs = four(rope_c[:, 0:heads * HD]), four(rope_s[:, 0:heads * HD])
                    if kind == "q":
                        outs = [four(qn[:, n % 2, 0:heads * HD])]
                    else:
                        kd = kdup[:, t, :].rearrange("p (h c a d) -> p h c a d", c=2, a=2, d=HD // 2)
                        outs = [kd[:, :, c, :, :] for c in range(2)]
                    for o in outs:
                        own.inc(nc.gpsimd.tensor_tensor(o[:, :, 0, :], rc[:, :, 0, :], rs[:, :, 1, :], ALU.subtract))
                        last = nc.gpsimd.tensor_tensor(o[:, :, 1, :], rc[:, :, 1, :], rs[:, :, 0, :], ALU.add)
                        if o is not outs[-1]:
                            own.inc(last)
                    last.then_inc(qn_ready, 1)
                    own.wait()
                    pool.wait_ge(qn_ready, n + 1)

                for h in range(HEADS):
                    g = HEADS * L + h
                    if m == REL and h in (4, 8):
                        pool.wait_ge(s_min, 2 * g)
                        load_bias(h // 4 + 1)
                    pool.wait_ge(rden_ready, g + 1)
                    nc.gpsimd.tensor_scalar(sc[:, h % SC, 0:P], sc[:, h % SC, 0:P], den[:, 0, h:h + 1], None,
                                            ALU.mult).then_inc(pn_first, 1)

                norm_rstd(3 * L + 1)
                if L + 1 < DEPTH:
                    load_gain(3 * L + 3)

                def up_unit(u, slot, half, k):
                    b = slot % 2
                    pool.wait_ge(silu_done, k + (FC * L + 1))
                    nc.gpsimd.tensor_tensor(gate_c[:, b, :], gate_c[:, b, :], up_c[:, b, :], ALU.mult).then_inc(prod_done, 1)
                    pool.wait_ge(gT_hi_ready, k + (FC * L + 1))
                    nc.gpsimd.tensor_tensor(gT_lo[:, k, :], gate_c[:, b, :], gT_hi[:, k, :].bitcast(F32), ALU.subtract).then_inc(gT_ready, 1)

                over_units(pool, FIRST_UP[L], FC, up_unit)
                norm_rstd(3 * L + 2)
                if L + 1 < DEPTH:
                    load_gain(3 * L + 4)

        @block.tensor
        def _(pe):
            def three(out_ap, l_hi, l_lo, r_hi, r_lo, start, stop):
                nc.tensor.matmul(out_ap, l_hi, r_hi, start=start, stop=False, skip_group_check=True)
                nc.tensor.matmul(out_ap, l_hi, r_lo, start=False, stop=False, skip_group_check=True)
                return nc.tensor.matmul(out_ap, l_lo, r_hi, start=False, stop=stop, skip_group_check=True)

            def transpose_tok(n, t):
                pe.wait_ge(tok_ready, 2 * n + t + 1)
                for b in range(2):
                    for c in range(4):
                        k = 4 * b + c
                        last = nc.tensor.transpose(acc[2 * t + b][:, c * P:(c + 1) * P],
                                                   tok[:, t, k * P:(k + 1) * P], ident[:])
                    last.then_inc(tr_done, 1)

            def rows_unit(first, k, count, t, left_hi, left_lo, banks):
                slot = (first + k) % RING
                ts = slice(t * P, (t + 1) * P)
                for j in range(2):
                    c = 2 * k + j
                    for l, ws in ((left_hi, (w_hi, w_lo)), (left_lo, (w_hi,))):
                        for w in ws:
                            for b in range(2):
                                col = j * D + b * 512
                                last = nc.tensor.matmul(
                                    banks[2 * t + b][:, :], l[:, c, ts], w[:, slot, col:col + 512],
                                    start=(c == 0 and l is left_hi and w is w_hi),
                                    stop=(c == 2 * count - 1 and l is left_lo), skip_group_check=True)
                return last

            def wait_unit(u):
                pe.wait_ge(lo_ready, u * 2 + 2)

            def second_pass(first, ks, count, left_hi, left_lo, next_norm):
                for k in ks:
                    if k == ks[-1] and next_norm is not None:
                        transpose_tok(next_norm, 0)
                    rows_unit(first, k, count, 1, left_hi, left_lo, acc).then_inc(unit_used, 1)

            pe.wait_ge(ident_landed, 16)
            transpose_tok(0, 0)
            for L in range(DEPTH):
                m = MIXER[L]
                item0 = FIRST_ITEM[L]
                n0 = 3 * L

                def in_unit(i, g, u, t):
                    kind, _, units = BLOCKS[m][i]
                    width = 256 if kind == "kv" else 512
                    chunks = KC // units
                    ts = slice(t * P, (t + 1) * P)
                    for c in range(chunks):
                        k = chunks * g + c
                        col = slice(c * width, (c + 1) * width)
                        last = three(acc[2 * t + i % 2][:, 0:width], hT_hi[:, k, ts], hT_lo[:, k, ts],
                                     w_hi[:, u % RING, col], w_lo[:, u % RING, col], k == 0, k == KC - 1)
                    return last

                def transpose_items(pair):
                    for i in (2 * pair, 2 * pair + 1):
                        n = item0 + i
                        pe.wait_ge(qn_ready, n + 1)
                        if n >= 2:
                            pe.wait_ge(qkT_ready, n - 1)
                        t = ITEMS[m][i][1]
                        doubled = item_place(m, i)[3] == 2
                        for c in range(2 if doubled else 4):
                            src = kdup[:, t, c * P:(c + 1) * P] if doubled else qn[:, n % 2, c * P:(c + 1) * P]
                            last = nc.tensor.transpose(aux[n % 2][:, c * P:(c + 1) * P], src, ident[:])
                        last.then_inc(qk_tr, 1)

                pair_units = [(i, g) for i in range(2) for g in range(BLOCKS[m][i][2])]
                pe.wait_ge(hT_ready, 4 * n0 + 2)
                for t in range(TT):
                    if t == 1:
                        pe.wait_ge(hT_ready, 4 * n0 + 4)
                    for j, (i, g) in enumerate(pair_units):
                        u = FIRST_IN[L] + j
                        if t == 0:
                            wait_unit(u)
                            if j == (len(pair_units) - 1 if L else 1):
                                transpose_tok(n0, 1)
                        last = in_unit(i, g, u, t)
                        ends = g == BLOCKS[m][i][2] - 1
                        if t == 0 and ends:
                            last.then_inc(in_done, 1)
                        if t == 1:
                            last.then_inc(unit_used, 1)
                transpose_items(0)
                if m == FOX:
                    k3 = L // 3
                    pe.wait_ge(wf_ready, 1)
                    for k in range(KC):
                        last = three(aux[3][0:HEADS, 0:SEQ], wf_hi[:, k3, k, :], wf_lo[:, k3, k, :],
                                     hT_hi[:, k, :], hT_lo[:, k, :], k == 0, k == KC - 1)
                    last.then_inc(f_done, 1)
                u = FIRST_IN[L] + len(pair_units)
                for i in range(2, len(BLOCKS[m])):
                    if BLOCKS[m][i - 2][0] != "v":
                        pe.wait_ge(qn_raw, item0 + ITEMS[m].index((i - 2, 1)) + 1)
                    if "v" in BLOCKS[m][i - 2][0]:
                        pe.wait_ge(v_ready, FIRST_V[L] + VS[m].index((i - 2, 1)) + 1)
                    for g in range(BLOCKS[m][i][2]):
                        wait_unit(u)
                        for t in range(TT):
                            last = in_unit(i, g, u, t)
                            if g == BLOCKS[m][i][2] - 1 and t == 0:
                                last.then_inc(in_done, 1)
                        last.then_inc(unit_used, 1)
                        u += 1
                    if 2 * (i - 1) + 1 < len(ITEMS[m]):
                        transpose_items(i - 1)
                if m == SWA:
                    transpose_items(2)
                if m == FOX:
                    pe.wait_ge(sel_ready, 1)
                    pe.wait_ge(cum_ready, L // 3 + 1)
                pe.wait_ge(qkT_ready, item0 + len(ITEMS[m]))
                pe.wait_ge(zero_ready, 2 * (L + 1))

                def scores(h):
                    g = HEADS * L + h
                    if h >= 2:
                        pe.wait_ge(s_min, 2 * (g - 1))
                    r = slice((h % 2) * HD, (h % 2) * HD + HD)
                    kp = h // 8 if m == SWA else h // 2
                    for qb in range(2):
                        dst = aux[h % 2][:, qb * SEQ:(qb + 1) * SEQ]
                        ts = slice(qb * P, (qb + 1) * P)
                        last = three(dst, qT_hi[r, h // 2, ts], qT_lo[r, h // 2, ts], kT_hi[r, kp, :], kT_lo[r, kp, :],
                                     True, m != FOX)
                        if m == FOX:
                            last = nc.tensor.matmul(dst, sel[:, h:h + 1].to_broadcast([P, P]), cum[:, :],
                                                    start=False, stop=True, skip_group_check=True)
                    last.then_inc(s_done, 1)

                def transpose_p(h):
                    g = HEADS * L + h
                    pe.wait_ge(pn_first, g + 1)
                    pe.wait_ge(pn_second, g + 1)
                    if h >= 2:
                        pe.wait_ge(pt_ready, g - 1)
                    for at, c in ((1, 2), (2, 0), (3, 1)):
                        last = nc.tensor.transpose(aux[2 + h % 2][:, at * P:(at + 1) * P], sc[:, h % SC, c * P:(c + 1) * P], ident[:])
                    last.then_inc(pt_done, 1)

                def values(h):
                    g = HEADS * L + h
                    pair = h // 2
                    pe.wait_ge(pt_ready, g + 1)
                    if h == 0:
                        pe.wait_ge(v_ready, FIRST_V[L] + len(VS[m]))
                    if h % 2 == 0 and pair >= 2:
                        pe.wait_ge(o_ready, HEADS // 2 * L + pair - 1)
                    vc = (h // 8 if m == SWA else pair) * P
                    dst = acc[2 + pair % 2][:, (h % 2) * SEQ:(h % 2 + 1) * SEQ]
                    for kc in range(TT):
                        ps = slice(SEQ * (1 - kc), SEQ * (2 - kc))
                        last = three(dst, v_hi[:, kc, vc:vc + P], v_lo[:, kc, vc:vc + P],
                                     pT_hi[:, h % 2, ps], pT_lo[:, h % 2, ps], kc == 0, kc == TT - 1)
                    last.then_inc(pv_done, 1)

                def o_unit(k):
                    wait_unit(FIRST_O[L] + k)
                    pe.wait_ge(o_ready, HEADS // 2 * L + 2 * k + 2)
                    return rows_unit(FIRST_O[L], k, ROW_UNITS, 0, hT_hi, hT_lo, acc)

                for h in range(HEADS + 3):
                    if h < HEADS:
                        scores(h)
                    if 2 <= h < HEADS + 2:
                        transpose_p(h - 2)
                    if h >= 3:
                        values(h - 3)
                    if h in (9, 13, 17):
                        o_unit((h - 9) // 4)
                o_unit(ROW_UNITS - 1).then_inc(tile_done, 1)
                second_pass(FIRST_O[L], list(range(ROW_UNITS)), ROW_UNITS, hT_hi, hT_lo, n0 + 1)

                wait_unit(FIRST_PLE[L])
                pe.wait_ge(ps_ready, L + 1)
                for t in range(TT):
                    last = rows_unit(FIRST_PLE[L], 0, 1, t, p_hi, p_lo, aux)
                last.then_inc(unit_used, 1)
                transpose_tok(n0 + 1, 1)
                pe.wait_ge(hT_ready, 4 * (n0 + 1) + 4)
                pe.wait_ge(pp_first, 2 * (L + 1))
                pe.wait_ge(pp_second, 2 * (L + 1))

                def up_unit(u, slot, half, k):
                    wait_unit(u)
                    if not isinstance(k, int) or FC * L + k >= RING:
                        pe.wait_ge(conv_done, k + (FC * L + 1 - RING))
                    for side in range(2):
                        for c in range(KC):
                            col = slice(c * 256 + side * P, c * 256 + (side + 1) * P)
                            last = three(aux[slot][:, side * SEQ:(side + 1) * SEQ], w_hi[:, slot, col], w_lo[:, slot, col],
                                         hT_hi[:, c, :], hT_lo[:, c, :], c == 0, c == KC - 1)
                    last.then_inc(unit_used, 1)

                over_units(pe, FIRST_UP[L], FC, up_unit, peel=L == 0)
                head = DOWN_UNITS - DOWN_TAIL
                tail = list(range(head, DOWN_UNITS))
                for k in range(head):
                    wait_unit(FIRST_DOWN[L] + k)
                    pe.wait_ge(gT_ready, FC * L + 2 * k + 2)
                    for t in range(TT):
                        last = rows_unit(FIRST_DOWN[L], k, DOWN_UNITS, t, gT_hi, gT_lo, acc)
                    last.then_inc(unit_used, 1)
                for k in tail:
                    wait_unit(FIRST_DOWN[L] + k)
                    pe.wait_ge(gT_ready, FC * L + 2 * k + 2)
                    last = rows_unit(FIRST_DOWN[L], k, DOWN_UNITS, 0, gT_hi, gT_lo, acc)
                last.then_inc(tile_done, 1)
                second_pass(FIRST_DOWN[L], tail, DOWN_UNITS, gT_hi, gT_lo, n0 + 2)
                pe.wait_ge(hT_ready, 4 * (n0 + 2) + 2)
                for k in range(ROW_UNITS):
                    wait_unit(FIRST_GATE[L] + k)
                    if k == 2:
                        transpose_tok(n0 + 2, 1)
                    last = rows_unit(FIRST_GATE[L], k, ROW_UNITS, 0, hT_hi, hT_lo, acc)
                last.then_inc(tile_done, 1)
                pe.wait_ge(hT_ready, 4 * (n0 + 2) + 4)
                second_pass(FIRST_GATE[L], list(range(ROW_UNITS)), ROW_UNITS, hT_hi, hT_lo, n0 + 3 if L + 1 < DEPTH else None)


def in_units(w):
    w = w.reshape(KC, P, w.shape[1])
    out = []
    if w.shape[2] % 512:
        out.append(w[:, :, -256:].transpose(1, 0, 2).reshape(P, UNIT))
    for c in range(0, w.shape[2] - 511, 512):
        for g in range(2):
            out.append(w[4 * g:4 * g + 4, :, c:c + 512].transpose(1, 0, 2).reshape(P, UNIT))
    return out


def row_units(w):
    w = w.reshape(w.shape[0] // (2 * P), 2, P, D)
    return [a.transpose(1, 0, 2).reshape(P, UNIT) for a in w]


def up_units(w):
    w = w.reshape(KC, P, 2, FC, P)
    return [w[:, :, :, j].transpose(1, 0, 2, 3).reshape(P, UNIT) for j in range(FC)]


def constants():
    t, s = np.arange(P)[:, None], np.arange(SEQ)[None, :]
    c = np.zeros((P, C_END), np.float32)
    both = np.concatenate([np.where(s[:, :P] > t, BIG, 0.0), np.where(s > t + P, BIG, 0.0)], 1)
    c[:, C_MASKA:C_MASKC] = both
    seen = lambda q, k: (k // CHUNK <= q // CHUNK) & (k // CHUNK >= q // CHUNK - 1)
    c[:, C_MASKC:C_MASKB] = np.where(np.concatenate([seen(t, s[:, :P]), seen(t + P, s)], 1), 0.0, BIG)
    c[:CHUNK, C_MASKB:C_SEL] = BIG
    c[:HEADS, C_SEL:C_COS] = c[CUM_LO:CUM_LO + HEADS, C_SEL:C_COS] = np.eye(HEADS)
    half = HD // 2
    inv = np.float32(10000.0) ** (-np.arange(half, dtype=np.float32) / np.float32(half))
    ang = np.arange(SEQ, dtype=np.float32)[:, None] * inv[None, :]
    tiles = lambda a: a.reshape(TT, P, half).transpose(1, 0, 2).reshape(P, TT * half)
    c[:, C_COS:C_SIN], c[:, C_SIN:C_END] = tiles(np.cos(ang)), tiles(np.sin(ang))
    return c


def kernel(**inputs):
    import concourse.bacc as bacc
    from concourse.bass_utils import run_bass_kernel_spmd

    a = {k: np.asarray(val) for k, val in inputs.items()}
    units = []
    for L, m in enumerate(MIXER):
        w_in = a["w_in_" + "abc"[m]][L // 3]
        w_in = w_in[:, :3 * D] if m == FOX else w_in
        units += in_units(w_in) + row_units(a["w_o"][L]) + row_units(a["w_ple_proj"][L]) + up_units(a["w_up"][L])
        units += row_units(a["w_down"][L]) + row_units(a["w_ple_gate"][L])
    heads = [np.stack([a[f"qn_{'abc'[m]}"][L // 3], a[f"kn_{'abc'[m]}"][L // 3]]) for L, m in enumerate(MIXER)]
    taps = np.concatenate([a["conv_w"], a["conv_b"][:, None]], 1)
    taps = taps.reshape(DEPTH, 4, 2, FC, P).transpose(4, 0, 3, 2, 1).reshape(P, DEPTH, FC, 8)
    dist = np.clip(P + np.arange(P)[:, None] - np.arange(SEQ)[None, :], -P, P) + P
    arrays = {
        "weights": np.stack(units).reshape(UNITS, P, 2, HALF).transpose(0, 2, 1, 3).reshape(2 * UNITS, P, HALF),
        "x_in": a["x"][0],
        "p_in": a["p"][:, 0].reshape(DEPTH, SEQ, 2, P).transpose(0, 3, 2, 1),
        "gains": np.stack([a[k][L] for L in range(DEPTH) for k in ("attn_norm", "ffn_norm", "ple_norm")]),
        "smalls": np.concatenate([np.stack(heads).ravel(), a["sinks"].ravel()]),
        "bf_in": a["b_f"].T,
        "conv": taps,
        "wf_in": a["w_in_a"][:, :, 3 * D:].reshape(2, KC, P, HEADS).transpose(2, 0, 1, 3),
        "rel_in": a["rel_bias"][0][dist].transpose(0, 2, 1),
        "ident_in": np.eye(P, dtype=np.float32),
        "consts_in": constants(),
    }
    nc = bacc.Bacc("TRN2", target_bir_lowering=False, num_devices=1)
    arrays = {k: np.ascontiguousarray(val) for k, val in arrays.items()}
    args = {k: nc.dram_tensor(k, val.shape, F32, kind="ExternalInput").ap() for k, val in arrays.items()}
    out = nc.dram_tensor("out", (SEQ, D), F32, kind="ExternalOutput").ap()
    trunk(nc, out=out, **args)
    r = run_bass_kernel_spmd(nc, [arrays], core_ids=[0])
    return r.results[0]["out"].reshape(1, SEQ, D)
```
